# Optimizing a Trainium2 kernel written in Bass

```python
import math
import jax
import jax.numpy as jnp
from jax import lax
import numpy as np
import jax, jax.numpy as jnp

D_MODEL = 1024
BATCH = 1
SEQ = 256
DEPTH = 2

N_HEADS = 8
N_KV_HEADS = 2
HEAD_DIM = 64
Q_PER_KV = N_HEADS // N_KV_HEADS
ATTN_WIDTH = N_HEADS * HEAD_DIM
KV_WIDTH = N_KV_HEADS * HEAD_DIM
N_BRANCH = 3
CMP_LEN = 32
CMP_STRIDE = 16
CMP_HIDDEN = 128
SEL_LEN = 64
SEL_TOPK = 16
N_LOCAL_SEL = 2
WINDOW = 512
Q_BLOCK = 64
CONV_WIDTH = D_MODEL // 2
CONV_KERNEL = 31
MIX_WIDTH = ATTN_WIDTH + CONV_WIDTH
IN_WIDTH = ATTN_WIDTH + 6 * KV_WIDTH + N_HEADS * N_BRANCH + 2 * CONV_WIDTH
ROPE_THETA = 500000.0
ROPE_DIM = HEAD_DIM // 4
D_FF = 7 * D_MODEL // 2
N_EXPERTS = 8
TOP_K = 2
MOE_BLOCK = 128
EPS = 1e-6


def rms_norm(x, g):
    xf = x.astype(jnp.float32)
    y = xf * lax.rsqrt(jnp.mean(xf * xf, axis=-1, keepdims=True) + EPS)
    return (y * g.astype(jnp.float32)).astype(x.dtype)

def layer_norm(x, g, b):
    xf = x.astype(jnp.float32)
    xc = xf - jnp.mean(xf, axis=-1, keepdims=True)
    y = xc * lax.rsqrt(jnp.mean(xc * xc, axis=-1, keepdims=True) + EPS)
    return (y * g.astype(jnp.float32) + b.astype(jnp.float32)).astype(x.dtype)

def masked_softmax(s, mask):
    s = jnp.where(mask, s.astype(jnp.float32), -jnp.inf)
    m = jnp.max(s, axis=-1, keepdims=True)
    m = jnp.where(jnp.isfinite(m), m, 0.0)
    p = jnp.exp(s - m)
    return p / jnp.maximum(jnp.sum(p, axis=-1, keepdims=True), jnp.finfo(jnp.float32).tiny)

def rope_partial(x, pos):
    half = ROPE_DIM // 2
    inv_freq = ROPE_THETA ** (-2.0 * jnp.arange(half, dtype=jnp.float32) / ROPE_DIM)
    ang = pos.astype(jnp.float32)[..., None, None] * inv_freq
    cos, sin = jnp.cos(ang), jnp.sin(ang)
    xr = x[..., :ROPE_DIM].astype(jnp.float32)
    x1, x2 = xr[..., :half], xr[..., half:]
    rot = jnp.concatenate([x1 * cos - x2 * sin, x2 * cos + x1 * sin], axis=-1).astype(x.dtype)
    return jnp.concatenate([rot, x[..., ROPE_DIM:]], axis=-1)

def swiglu(x, wg, wu, wd):
    return (jax.nn.silu(x @ wg) * (x @ wu)) @ wd

def in_proj_split_points():
    sizes = [ATTN_WIDTH] + [KV_WIDTH] * 6 + [N_HEADS * N_BRANCH, 2 * CONV_WIDTH]
    return [int(v) for v in np.cumsum(sizes)[:-1]]

def n_cmp_blocks(s):
    return (s - CMP_LEN) // CMP_STRIDE + 1

def cmp_block_ends(s):
    return np.arange(n_cmp_blocks(s)) * CMP_STRIDE + CMP_LEN - 1

def selection_map(s):
    c0 = np.arange(n_cmp_blocks(s)) * CMP_STRIDE
    s0 = np.arange(s // SEL_LEN) * SEL_LEN
    ov = np.minimum(c0[:, None] + CMP_LEN, s0[None, :] + SEL_LEN) - np.maximum(c0[:, None], s0[None, :])
    return jnp.asarray(np.clip(ov, 0, None) / CMP_LEN, dtype=jnp.float32)

def compress_blocks(kv, pos_emb, w1, w2):
    b, s = kv.shape[0], kv.shape[1]
    n_cmp = n_cmp_blocks(s)
    idx = np.arange(n_cmp)[:, None] * CMP_STRIDE + np.arange(CMP_LEN)[None, :]
    blocks = kv[:, idx] + pos_emb[None, None, :, None, :]
    blocks = blocks.transpose(0, 1, 3, 2, 4).reshape(b, n_cmp, N_KV_HEADS, CMP_LEN * HEAD_DIM)
    hid = jax.nn.gelu(jnp.einsum('bnkf,fh->bnkh', blocks, w1))
    return jnp.einsum('bnkh,hd->bnkd', hid, w2)

def nsa_attention(q, k_cmp, v_cmp, k_slc, v_slc, k_win, v_win, gates):
    b, s = q.shape[0], q.shape[1]
    n_sel = s // SEL_LEN
    top_n = min(SEL_TOPK, n_sel)
    scale = HEAD_DIM ** -0.5
    q = q.reshape(b, s, N_KV_HEADS, Q_PER_KV, HEAD_DIM)
    gates = gates.reshape(b, s, N_KV_HEADS, Q_PER_KV, N_BRANCH)
    cmp_end = jnp.asarray(cmp_block_ends(s))
    sel_map = selection_map(s)
    k_blk = k_slc.reshape(b, n_sel, SEL_LEN, N_KV_HEADS, HEAD_DIM).transpose(0, 3, 1, 2, 4)
    v_blk = v_slc.reshape(b, n_sel, SEL_LEN, N_KV_HEADS, HEAD_DIM).transpose(0, 3, 1, 2, 4)
    pad = ((0, 0), (WINDOW, 0), (0, 0), (0, 0))
    k_wpad = jnp.pad(k_win, pad)
    v_wpad = jnp.pad(v_win, pad)
    b_ix = jnp.arange(b)[:, None, None, None]
    h_ix = jnp.arange(N_KV_HEADS)[None, None, :, None]
    blk_ids = jnp.arange(n_sel)

    def query_block(c):
        t0 = c * Q_BLOCK
        t = t0 + jnp.arange(Q_BLOCK)
        qc = lax.dynamic_slice_in_dim(q, t0, Q_BLOCK, axis=1)
        gc = lax.dynamic_slice_in_dim(gates, t0, Q_BLOCK, axis=1)
        s_c = jnp.einsum('bqkgd,bnkd->bqkgn', qc, k_cmp) * scale
        mask_c = (cmp_end[None, :] <= t[:, None])[None, :, None, None, :]
        p_c = masked_softmax(s_c, mask_c)
        o_c = jnp.einsum('bqkgn,bnkd->bqkgd', p_c.astype(v_cmp.dtype), v_cmp)
        imp = jnp.einsum('bqkgn,nj->bqkj', p_c, sel_map)
        cur = (t // SEL_LEN)[:, None]
        causal_blk = blk_ids[None, :] <= cur
        forced = (blk_ids[None, :] == 0) | (causal_blk & (blk_ids[None, :] > cur - N_LOCAL_SEL))
        score = jnp.where(forced[None, :, None, :], jnp.inf,
                          jnp.where(causal_blk[None, :, None, :], imp, -jnp.inf))
        _, sel_idx = lax.top_k(score, top_n)
        k_sel = k_blk[b_ix, h_ix, sel_idx].reshape(b, Q_BLOCK, N_KV_HEADS, top_n * SEL_LEN, HEAD_DIM)
        v_sel = v_blk[b_ix, h_ix, sel_idx].reshape(b, Q_BLOCK, N_KV_HEADS, top_n * SEL_LEN, HEAD_DIM)
        tok = (sel_idx[..., None] * SEL_LEN + jnp.arange(SEL_LEN)).reshape(
            b, Q_BLOCK, N_KV_HEADS, 1, top_n * SEL_LEN)
        mask_s = tok <= t[None, :, None, None, None]
        s_s = jnp.einsum('bqkgd,bqkmd->bqkgm', qc, k_sel) * scale
        p_s = masked_softmax(s_s, mask_s)
        o_s = jnp.einsum('bqkgm,bqkmd->bqkgd', p_s.astype(v_sel.dtype), v_sel)
        k_w = lax.dynamic_slice_in_dim(k_wpad, t0, WINDOW + Q_BLOCK, axis=1)
        v_w = lax.dynamic_slice_in_dim(v_wpad, t0, WINDOW + Q_BLOCK, axis=1)
        src = t0 - WINDOW + jnp.arange(WINDOW + Q_BLOCK)
        mask_w = ((src[None, :] >= 0) & (src[None, :] <= t[:, None])
                  & (src[None, :] > t[:, None] - WINDOW))[None, :, None, None, :]
        s_w = jnp.einsum('bqkgd,bwkd->bqkgw', qc, k_w) * scale
        p_w = masked_softmax(s_w, mask_w)
        o_w = jnp.einsum('bqkgw,bwkd->bqkgd', p_w.astype(v_w.dtype), v_w)
        return gc[..., 0:1] * o_c + gc[..., 1:2] * o_s + gc[..., 2:3] * o_w

    out = lax.map(query_block, jnp.arange(s // Q_BLOCK))
    return out.transpose(1, 0, 2, 3, 4, 5).reshape(b, s, ATTN_WIDTH)

def conformer_conv(u, conv_w, conv_b, ln_g, ln_b):
    a, g = jnp.split(u, 2, axis=-1)
    h = a * jax.nn.sigmoid(g)
    h = jnp.pad(h, ((0, 0), (CONV_KERNEL - 1, 0), (0, 0)))
    y = lax.conv_general_dilated(h, conv_w[:, None, :], window_strides=(1,), padding='VALID',
                                 dimension_numbers=('NWC', 'WIO', 'NWC'),
                                 feature_group_count=CONV_WIDTH)
    y = y + conv_b
    return jax.nn.silu(layer_norm(y, ln_g, ln_b))

def moe_swiglu(h, router, wg, wu, wd):
    b, s, d = h.shape
    n_tok = b * s
    xt = h.reshape(n_tok, d)
    logits = (xt @ router).astype(jnp.float32)
    top_logit, top_e = lax.top_k(logits, TOP_K)
    gate = jax.nn.softmax(top_logit, axis=-1)
    n_asg = n_tok * TOP_K
    e_flat = top_e.reshape(n_asg)
    tok_flat = jnp.broadcast_to(jnp.arange(n_tok)[:, None], (n_tok, TOP_K)).reshape(n_asg)
    g_flat = gate.reshape(n_asg)
    order = jnp.argsort(e_flat)
    e_s, tok_s, g_s = e_flat[order], tok_flat[order], g_flat[order]
    counts = jnp.bincount(e_flat, length=N_EXPERTS)
    padded = (counts + MOE_BLOCK - 1) // MOE_BLOCK * MOE_BLOCK
    start = jnp.cumsum(counts) - counts
    pend = jnp.cumsum(padded)
    pstart = pend - padded
    dest = pstart[e_s] + jnp.arange(n_asg) - start[e_s]
    n_blocks = -(-n_asg // MOE_BLOCK) + N_EXPERTS
    n_slots = n_blocks * MOE_BLOCK
    slot_tok = jnp.full((n_slots,), n_tok, jnp.int32).at[dest].set(tok_s.astype(jnp.int32))
    slot_gate = jnp.zeros((n_slots,), jnp.float32).at[dest].set(g_s)
    blk_e = jnp.clip(jnp.searchsorted(pend, jnp.arange(n_blocks) * MOE_BLOCK, side='right'),
                     0, N_EXPERTS - 1)
    x_pad = jnp.concatenate([xt, jnp.zeros((1, d), xt.dtype)], axis=0)
    xs = x_pad[slot_tok].reshape(n_blocks, MOE_BLOCK, d)

    def expert_block(args):
        xb, e = args
        return swiglu(xb, wg[e], wu[e], wd[e])

    ys = lax.map(expert_block, (xs, blk_e)).reshape(n_slots, d)
    ys = ys * slot_gate[:, None].astype(ys.dtype)
    out = jax.ops.segment_sum(ys, slot_tok, num_segments=n_tok + 1)[:n_tok]
    return out.reshape(b, s, d)

def first_inputs(seed: int = 0) -> dict:
    key = jax.random.key(seed)
    keys = list(jax.random.split(key, 32))

    def nrm(i, shape, scale):
        return scale * jax.random.normal(keys[i], shape, jnp.float32)

    n_dense = (DEPTH + 1) // 2
    n_moe = DEPTH // 2
    x = nrm(0, (BATCH, SEQ, D_MODEL), 1.0)
    offsets = jax.random.randint(keys[1], (BATCH, 1), 0, 2048, dtype=jnp.int32)
    positions = offsets + jnp.arange(SEQ, dtype=jnp.int32)[None, :]
    return {
        "x": x,
        "positions": positions,
        "attn_norm_g": 1.0 + nrm(2, (DEPTH, D_MODEL), 0.02),
        "ffn_norm_g": 1.0 + nrm(3, (DEPTH, D_MODEL), 0.02),
        "w_in": nrm(4, (DEPTH, D_MODEL, IN_WIDTH), D_MODEL ** -0.5),
        "w_out": nrm(5, (DEPTH, MIX_WIDTH, D_MODEL), MIX_WIDTH ** -0.5),
        "q_norm_g": 1.0 + nrm(6, (DEPTH, HEAD_DIM), 0.02),
        "k_norm_g": 1.0 + nrm(7, (DEPTH, N_BRANCH, HEAD_DIM), 0.02),
        "cmp_pos_k": nrm(8, (DEPTH, CMP_LEN, HEAD_DIM), 0.1),
        "cmp_w1_k": nrm(9, (DEPTH, CMP_LEN * HEAD_DIM, CMP_HIDDEN), (CMP_LEN * HEAD_DIM) ** -0.5),
        "cmp_w2_k": nrm(10, (DEPTH, CMP_HIDDEN, HEAD_DIM), CMP_HIDDEN ** -0.5),
        "cmp_pos_v": nrm(11, (DEPTH, CMP_LEN, HEAD_DIM), 0.1),
        "cmp_w1_v": nrm(12, (DEPTH, CMP_LEN * HEAD_DIM, CMP_HIDDEN), (CMP_LEN * HEAD_DIM) ** -0.5),
        "cmp_w2_v": nrm(13, (DEPTH, CMP_HIDDEN, HEAD_DIM), CMP_HIDDEN ** -0.5),
        "conv_w": nrm(14, (DEPTH, CONV_KERNEL, CONV_WIDTH), CONV_KERNEL ** -0.5),
        "conv_b": nrm(15, (DEPTH, CONV_WIDTH), 0.02),
        "conv_ln_g": 1.0 + nrm(16, (DEPTH, CONV_WIDTH), 0.02),
        "conv_ln_b": nrm(17, (DEPTH, CONV_WIDTH), 0.02),
        "ffn_w_gate": nrm(18, (n_dense, D_MODEL, D_FF), D_MODEL ** -0.5),
        "ffn_w_up": nrm(19, (n_dense, D_MODEL, D_FF), D_MODEL ** -0.5),
        "ffn_w_down": nrm(20, (n_dense, D_FF, D_MODEL), D_FF ** -0.5),
        "moe_router": nrm(21, (n_moe, D_MODEL, N_EXPERTS), D_MODEL ** -0.5),
        "moe_w_gate": nrm(22, (n_moe, N_EXPERTS, D_MODEL, D_FF), D_MODEL ** -0.5),
        "moe_w_up": nrm(23, (n_moe, N_EXPERTS, D_MODEL, D_FF), D_MODEL ** -0.5),
        "moe_w_down": nrm(24, (n_moe, N_EXPERTS, D_FF, D_MODEL), D_FF ** -0.5),
    }

def first_block(x, positions, attn_norm_g, ffn_norm_g, w_in, w_out, q_norm_g, k_norm_g,
              cmp_pos_k, cmp_w1_k, cmp_w2_k, cmp_pos_v, cmp_w1_v, cmp_w2_v,
              conv_w, conv_b, conv_ln_g, conv_ln_b,
              ffn_w_gate, ffn_w_up, ffn_w_down,
              moe_router, moe_w_gate, moe_w_up, moe_w_down):
    b, s, _ = x.shape
    pos_cmp = positions[:, cmp_block_ends(s)]
    split_points = in_proj_split_points()
    for layer in range(DEPTH):
        h = rms_norm(x, attn_norm_g[layer])
        proj = jnp.einsum('bsd,de->bse', h, w_in[layer])
        q, k_c, v_c, k_s, v_s, k_w, v_w, g_logit, u = jnp.split(proj, split_points, axis=-1)
        q = rope_partial(rms_norm(q.reshape(b, s, N_HEADS, HEAD_DIM), q_norm_g[layer]), positions)
        kv_shape = (b, s, N_KV_HEADS, HEAD_DIM)
        k_cmp = compress_blocks(k_c.reshape(kv_shape), cmp_pos_k[layer], cmp_w1_k[layer], cmp_w2_k[layer])
        k_cmp = rope_partial(rms_norm(k_cmp, k_norm_g[layer, 0]), pos_cmp)
        v_cmp = compress_blocks(v_c.reshape(kv_shape), cmp_pos_v[layer], cmp_w1_v[layer], cmp_w2_v[layer])
        k_slc = rope_partial(rms_norm(k_s.reshape(kv_shape), k_norm_g[layer, 1]), positions)
        k_win = rope_partial(rms_norm(k_w.reshape(kv_shape), k_norm_g[layer, 2]), positions)
        gates = jax.nn.sigmoid(g_logit.astype(jnp.float32)).astype(x.dtype).reshape(b, s, N_HEADS, N_BRANCH)
        attn_out = nsa_attention(q, k_cmp, v_cmp, k_slc, v_s.reshape(kv_shape),
                                 k_win, v_w.reshape(kv_shape), gates)
        conv_out = conformer_conv(u, conv_w[layer], conv_b[layer], conv_ln_g[layer], conv_ln_b[layer])
        mixed = jnp.concatenate([attn_out, conv_out], axis=-1)
        x = x + jnp.einsum('bsm,md->bsd', mixed, w_out[layer])
        h = rms_norm(x, ffn_norm_g[layer])
        if layer % 2 == 0:
            i = layer // 2
            x = x + swiglu(h, ffn_w_gate[i], ffn_w_up[i], ffn_w_down[i])
        else:
            i = layer // 2
            x = x + moe_swiglu(h, moe_router[i], moe_w_gate[i], moe_w_up[i], moe_w_down[i])
    return x


MEM_LEN = 256
MLA_HEADS = 6
MLA_NOPE = 64
MLA_ROPE = 32
MLA_V = 64
MLA_Q_RANK = 256
MLA_KV_RANK = 128
ROPE_THETA_2 = 10000.0
DIFF_HEADS = 6
DIFF_HD = 32
MOBA_HEADS = 4
MOBA_HD = 64
MOBA_BLOCK = 256
MOBA_TOPK = 3
MOBA_Q_CHUNK = 32
Q_BLOCK_2 = 128
CROSS_HEADS = 4
CROSS_HD = D_MODEL // CROSS_HEADS
D_FF_2 = 4 * D_MODEL
NEG = -1e30
N_ALIBI = DIFF_HEADS + MOBA_HEADS

C_Q = MLA_Q_RANK
C_KV = MLA_KV_RANK
C_KR = MLA_ROPE
C_DIFF = DIFF_HEADS * 2 * DIFF_HD
C_MOBA = MOBA_HEADS * MOBA_HD
D_IN = C_Q + C_KV + C_KR + 3 * C_DIFF + 3 * C_MOBA
D_MIX = MLA_HEADS * MLA_V + DIFF_HEADS * 2 * DIFF_HD + MOBA_HEADS * MOBA_HD


def rmsnorm(x, g):
    xf = x.astype(jnp.float32)
    y = xf * lax.rsqrt(jnp.mean(xf * xf, axis=-1, keepdims=True) + EPS)
    return (y * g.astype(jnp.float32)).astype(x.dtype)

def alibi_slopes():
    return jnp.asarray([2.0 ** (-8.0 * (h + 1) / N_ALIBI) for h in range(N_ALIBI)], jnp.float32)

def apply_rope(x, pos):
    half = x.shape[-1] // 2
    inv = ROPE_THETA_2 ** (-jnp.arange(half, dtype=jnp.float32) / half)
    ang = pos.astype(jnp.float32)[:, None, :, None] * inv
    cos, sin = jnp.cos(ang), jnp.sin(ang)
    xf = x.astype(jnp.float32)
    x1, x2 = xf[..., :half], xf[..., half:]
    return jnp.concatenate([x1 * cos - x2 * sin, x1 * sin + x2 * cos], axis=-1).astype(x.dtype)

def to_heads(t, hd):
    B, S, _ = t.shape
    return t.reshape(B, S, -1, hd).transpose(0, 2, 1, 3)

def from_heads(t):
    B, H, S, d = t.shape
    return t.transpose(0, 2, 1, 3).reshape(B, S, H * d)

def sweep_query_blocks(body, B, H, S, dv):
    out = lax.map(body, jnp.arange(S // Q_BLOCK_2, dtype=jnp.int32) * Q_BLOCK_2)
    return jnp.moveaxis(out, 0, 2).reshape(B, H, S, dv)

def mla_causal_attention(q, k, v):
    B, H, S, dqk = q.shape
    scale = dqk ** -0.5
    kidx = jnp.arange(S)

    def body(start):
        qc = lax.dynamic_slice_in_dim(q, start, Q_BLOCK_2, axis=2)
        s = jnp.einsum('bhqd,bhkd->bhqk', qc, k, preferred_element_type=jnp.float32) * scale
        qidx = start + jnp.arange(Q_BLOCK_2)
        s = jnp.where(kidx[None, :] <= qidx[:, None], s, NEG)
        p = jax.nn.softmax(s, axis=-1)
        return jnp.einsum('bhqk,bhkd->bhqd', p.astype(v.dtype), v)

    return sweep_query_blocks(body, B, H, S, v.shape[-1])

def diff_causal_attention(q1, q2, k1, k2, v, pos, slopes, lam):
    B, H, S, d = q1.shape
    scale = d ** -0.5
    kidx = jnp.arange(S)

    def body(start):
        pq = lax.dynamic_slice_in_dim(pos, start, Q_BLOCK_2, axis=1)
        qidx = start + jnp.arange(Q_BLOCK_2)
        causal = kidx[None, :] <= qidx[:, None]
        dist = jnp.abs(pq[:, :, None] - pos[:, None, :]).astype(jnp.float32)
        bias = -slopes[None, :, None, None] * dist[:, None]

        def probs(qf, k):
            qc = lax.dynamic_slice_in_dim(qf, start, Q_BLOCK_2, axis=2)
            s = jnp.einsum('bhqd,bhkd->bhqk', qc, k, preferred_element_type=jnp.float32) * scale + bias
            return jax.nn.softmax(jnp.where(causal, s, NEG), axis=-1)

        p = probs(q1, k1) - lam * probs(q2, k2)
        return jnp.einsum('bhqk,bhkd->bhqd', p.astype(v.dtype), v)

    return sweep_query_blocks(body, B, H, S, v.shape[-1])

def moba_causal_attention(q, k, v, pos, slopes):
    B, H, S, dh = q.shape
    NB = -(-S // MOBA_BLOCK)
    pad = NB * MOBA_BLOCK - S
    kb = jnp.pad(k, ((0, 0), (0, 0), (0, pad), (0, 0))).reshape(B, H, NB, MOBA_BLOCK, dh)
    vb = jnp.pad(v, ((0, 0), (0, 0), (0, pad), (0, 0))).reshape(B, H, NB, MOBA_BLOCK, dh)
    pb = jnp.pad(pos, ((0, 0), (0, pad)), mode='edge').reshape(B, NB, MOBA_BLOCK)
    kmean = jnp.mean(kb.astype(jnp.float32), axis=3)
    K = min(MOBA_TOPK, NB)
    scale = dh ** -0.5
    bi = jnp.arange(B)[:, None, None, None]
    hi = jnp.arange(H)[None, :, None, None]
    m5 = slopes[None, :, None, None, None]

    def body(start):
        qc = lax.dynamic_slice_in_dim(q, start, MOBA_Q_CHUNK, axis=2)
        pq = lax.dynamic_slice_in_dim(pos, start, MOBA_Q_CHUNK, axis=1)
        qidx = start + jnp.arange(MOBA_Q_CHUNK)
        ob = start // MOBA_BLOCK
        gate = jnp.einsum('bhqd,bhnd->bhqn', qc.astype(jnp.float32), kmean)
        gate = jnp.where(jnp.arange(NB) < ob, gate, NEG)
        _, sel = lax.top_k(gate, K)
        valid = jnp.arange(K) < ob
        kg = kb[bi, hi, sel]
        vg = vb[bi, hi, sel]
        pg = pb[bi, sel]
        s_sel = jnp.einsum('bhqd,bhqkjd->bhqkj', qc, kg, preferred_element_type=jnp.float32) * scale
        s_sel = s_sel - m5 * jnp.abs(pq[:, None, :, None, None] - pg).astype(jnp.float32)
        s_sel = jnp.where(valid[None, None, None, :, None], s_sel, NEG)
        s_sel = s_sel.reshape(B, H, MOBA_Q_CHUNK, K * MOBA_BLOCK)
        ko = lax.dynamic_index_in_dim(kb, ob, axis=2, keepdims=False)
        vo = lax.dynamic_index_in_dim(vb, ob, axis=2, keepdims=False)
        po = lax.dynamic_index_in_dim(pb, ob, axis=1, keepdims=False)
        s_own = jnp.einsum('bhqd,bhjd->bhqj', qc, ko, preferred_element_type=jnp.float32) * scale
        s_own = s_own - slopes[None, :, None, None] * jnp.abs(pq[:, None, :, None] - po[:, None, None, :]).astype(jnp.float32)
        kidx = ob * MOBA_BLOCK + jnp.arange(MOBA_BLOCK)
        s_own = jnp.where(kidx[None, :] <= qidx[:, None], s_own, NEG)
        p = jax.nn.softmax(jnp.concatenate([s_sel, s_own], axis=-1), axis=-1).astype(v.dtype)
        p_sel = p[..., :K * MOBA_BLOCK].reshape(B, H, MOBA_Q_CHUNK, K, MOBA_BLOCK)
        return (jnp.einsum('bhqkj,bhqkjd->bhqd', p_sel, vg)
                + jnp.einsum('bhqj,bhjd->bhqd', p[..., K * MOBA_BLOCK:], vo))

    out = lax.map(body, jnp.arange(S // MOBA_Q_CHUNK, dtype=jnp.int32) * MOBA_Q_CHUNK)
    return jnp.moveaxis(out, 0, 2).reshape(B, H, S, dh)

def hybrid_mixer(n, pos, layer_idx, w_in, q_norm, w_uq, kv_norm, w_ukv,
                 lq1, lk1, lq2, lk2, sub_norm, w_out):
    B, S, _ = n.shape
    proj = n @ w_in
    cuts = [int(c) for c in np.cumsum([C_Q, C_KV, C_KR, C_DIFF, C_DIFF, C_DIFF, C_MOBA, C_MOBA])]
    c_q, c_kv, k_r, dq, dk, dv, mq, mk, mv = jnp.split(proj, cuts, axis=-1)
    slopes = alibi_slopes()

    qh = to_heads(rmsnorm(c_q, q_norm) @ w_uq, MLA_NOPE + MLA_ROPE)
    kvh = to_heads(rmsnorm(c_kv, kv_norm) @ w_ukv, MLA_NOPE + MLA_V)
    q_rope = apply_rope(qh[..., MLA_NOPE:], pos)
    k_rope = apply_rope(k_r[:, None], pos)
    q_a = jnp.concatenate([qh[..., :MLA_NOPE], q_rope], axis=-1)
    k_a = jnp.concatenate([kvh[..., :MLA_NOPE],
                           jnp.broadcast_to(k_rope, (B, MLA_HEADS, S, MLA_ROPE))], axis=-1)
    o_a = mla_causal_attention(q_a, k_a, kvh[..., MLA_NOPE:])

    dqh, dkh, dvh = to_heads(dq, 2 * DIFF_HD), to_heads(dk, 2 * DIFF_HD), to_heads(dv, 2 * DIFF_HD)
    lam_init = 0.8 - 0.6 * math.exp(-0.3 * layer_idx)
    lam = (jnp.exp(jnp.sum(lq1.astype(jnp.float32) * lk1.astype(jnp.float32)))
           - jnp.exp(jnp.sum(lq2.astype(jnp.float32) * lk2.astype(jnp.float32))) + lam_init)
    o_b = diff_causal_attention(dqh[..., :DIFF_HD], dqh[..., DIFF_HD:],
                                dkh[..., :DIFF_HD], dkh[..., DIFF_HD:],
                                dvh, pos, slopes[:DIFF_HEADS], lam)
    o_b = rmsnorm(o_b, sub_norm) * (1.0 - lam_init)

    o_c = moba_causal_attention(to_heads(mq, MOBA_HD), to_heads(mk, MOBA_HD),
                                to_heads(mv, MOBA_HD), pos, slopes[DIFF_HEADS:])

    o = jnp.concatenate([from_heads(o_a), from_heads(o_b), from_heads(o_c)], axis=-1)
    return o @ w_out

def memory_cross_attention(n, mem_n, wq, wkv, wo):
    q = to_heads(n @ wq, CROSS_HD)
    kv = mem_n @ wkv
    k = to_heads(kv[..., :D_MODEL], CROSS_HD)
    v = to_heads(kv[..., D_MODEL:], CROSS_HD)
    s = jnp.einsum('bhqd,bhmd->bhqm', q, k, preferred_element_type=jnp.float32) * (CROSS_HD ** -0.5)
    p = jax.nn.softmax(s, axis=-1).astype(v.dtype)
    return from_heads(jnp.einsum('bhqm,bhmd->bhqd', p, v)) @ wo

def squared_relu_mlp(n, w1, w2):
    return jnp.square(jax.nn.relu(n @ w1)) @ w2

def second_inputs(seed: int = 0) -> dict:
    key = jax.random.key(seed)
    k = jax.random.split(key, 24)
    L = DEPTH
    f32 = jnp.float32
    nrm = lambda kk, shape, scale: jax.random.normal(kk, shape, f32) * scale
    gain = lambda kk, shape: 1.0 + 0.02 * jax.random.normal(kk, shape, f32)
    offset = jax.random.randint(k[2], (BATCH, 1), 0, 1024, dtype=jnp.int32)
    positions = offset + jnp.arange(SEQ, dtype=jnp.int32)[None, :]
    return {
        "x": nrm(k[0], (BATCH, SEQ, D_MODEL), 1.0),
        "mem": nrm(k[1], (BATCH, MEM_LEN, D_MODEL), 1.0),
        "positions": positions,
        "attn_norm": gain(k[3], (L, D_MODEL)),
        "w_in": nrm(k[4], (L, D_MODEL, D_IN), D_MODEL ** -0.5),
        "mla_q_norm": gain(k[5], (L, MLA_Q_RANK)),
        "mla_w_uq": nrm(k[6], (L, MLA_Q_RANK, MLA_HEADS * (MLA_NOPE + MLA_ROPE)), MLA_Q_RANK ** -0.5),
        "mla_kv_norm": gain(k[7], (L, MLA_KV_RANK)),
        "mla_w_ukv": nrm(k[8], (L, MLA_KV_RANK, MLA_HEADS * (MLA_NOPE + MLA_V)), MLA_KV_RANK ** -0.5),
        "diff_lambda_q1": nrm(k[9], (L, DIFF_HD), 0.1),
        "diff_lambda_k1": nrm(k[10], (L, DIFF_HD), 0.1),
        "diff_lambda_q2": nrm(k[11], (L, DIFF_HD), 0.1),
        "diff_lambda_k2": nrm(k[12], (L, DIFF_HD), 0.1),
        "diff_sub_norm": gain(k[13], (L, 2 * DIFF_HD)),
        "w_out": nrm(k[14], (L, D_MIX, D_MODEL), D_MIX ** -0.5),
        "cross_norm": gain(k[15], (L, D_MODEL)),
        "mem_norm": gain(k[16], (L, D_MODEL)),
        "cross_wq": nrm(k[17], (L, D_MODEL, D_MODEL), D_MODEL ** -0.5),
        "cross_wkv": nrm(k[18], (L, D_MODEL, 2 * D_MODEL), D_MODEL ** -0.5),
        "cross_wo": nrm(k[19], (L, D_MODEL, D_MODEL), D_MODEL ** -0.5),
        "mlp_norm": gain(k[20], (L, D_MODEL)),
        "mlp_w1": nrm(k[21], (L, D_MODEL, D_FF_2), D_MODEL ** -0.5),
        "mlp_w2": nrm(k[22], (L, D_FF_2, D_MODEL), D_FF_2 ** -0.5),
        "final_norm": gain(k[23], (D_MODEL,)),
    }

def second_block(x, mem, positions, attn_norm, w_in, mla_q_norm, mla_w_uq, mla_kv_norm, mla_w_ukv,
              diff_lambda_q1, diff_lambda_k1, diff_lambda_q2, diff_lambda_k2, diff_sub_norm, w_out,
              cross_norm, mem_norm, cross_wq, cross_wkv, cross_wo, mlp_norm, mlp_w1, mlp_w2, final_norm):
    h = x
    for l in range(DEPTH):
        h = h + hybrid_mixer(rmsnorm(h, attn_norm[l]), positions, l, w_in[l],
                             mla_q_norm[l], mla_w_uq[l], mla_kv_norm[l], mla_w_ukv[l],
                             diff_lambda_q1[l], diff_lambda_k1[l], diff_lambda_q2[l], diff_lambda_k2[l],
                             diff_sub_norm[l], w_out[l])
        h = h + memory_cross_attention(rmsnorm(h, cross_norm[l]), rmsnorm(mem, mem_norm[l]),
                                       cross_wq[l], cross_wkv[l], cross_wo[l])
        h = h + squared_relu_mlp(rmsnorm(h, mlp_norm[l]), mlp_w1[l], mlp_w2[l])
    return rmsnorm(h, final_norm)


def setup_inputs(seed=0):
    out = dict(first_inputs(seed))
    for name, value in second_inputs(seed + 1).items():
        if name != "x":
            out[name + "_2"] = value
    return out


def reference(
    x, positions, attn_norm_g, ffn_norm_g, w_in, w_out, q_norm_g, k_norm_g, cmp_pos_k, cmp_w1_k,
    cmp_w2_k, cmp_pos_v, cmp_w1_v, cmp_w2_v, conv_w, conv_b, conv_ln_g, conv_ln_b, ffn_w_gate,
    ffn_w_up, ffn_w_down, moe_router, moe_w_gate, moe_w_up, moe_w_down, mem_2, positions_2,
    attn_norm_2, w_in_2, mla_q_norm_2, mla_w_uq_2, mla_kv_norm_2, mla_w_ukv_2, diff_lambda_q1_2,
    diff_lambda_k1_2, diff_lambda_q2_2, diff_lambda_k2_2, diff_sub_norm_2, w_out_2,
    cross_norm_2, mem_norm_2, cross_wq_2, cross_wkv_2, cross_wo_2, mlp_norm_2, mlp_w1_2,
    mlp_w2_2, final_norm_2,
):
    x = first_block(
        x, positions, attn_norm_g, ffn_norm_g, w_in, w_out, q_norm_g, k_norm_g, cmp_pos_k,
        cmp_w1_k, cmp_w2_k, cmp_pos_v, cmp_w1_v, cmp_w2_v, conv_w, conv_b, conv_ln_g, conv_ln_b,
        ffn_w_gate, ffn_w_up, ffn_w_down, moe_router, moe_w_gate, moe_w_up, moe_w_down,
    )
    return second_block(
        x, mem_2, positions_2, attn_norm_2, w_in_2, mla_q_norm_2, mla_w_uq_2, mla_kv_norm_2,
        mla_w_ukv_2, diff_lambda_q1_2, diff_lambda_k1_2, diff_lambda_q2_2, diff_lambda_k2_2,
        diff_sub_norm_2, w_out_2, cross_norm_2, mem_norm_2, cross_wq_2, cross_wkv_2, cross_wo_2,
        mlp_norm_2, mlp_w1_2, mlp_w2_2, final_norm_2,
    )


_drawn_inputs = setup_inputs


def setup_inputs(seed=0):
    import zlib

    import numpy as np

    out = dict(_drawn_inputs(seed))
    spreads = {}
    factors = {'q_norm_g': 4.873,
     'k_norm_g': 3.84,
     'cmp_pos_k': 6.464,
     'attn_norm_2': 4.487,
     'mla_q_norm_2': 8.0,
     'mla_kv_norm_2': 8.0,
     'diff_lambda_q1_2': 5.278,
     'diff_lambda_k1_2': 8.0,
     'diff_sub_norm_2': 7.083,
     'cross_norm_2': 8.0,
     'mem_norm_2': 8.0,
     'mlp_norm_2': 2.89,
     'final_norm_2': 2.845}
    for name, (base, spread) in spreads.items():
        noise = np.random.default_rng([zlib.crc32(name.encode()), seed]).standard_normal(out[name].shape)
        drawn = base * np.exp(spread * noise) if base else spread * noise
        out[name] = jnp.asarray(drawn.astype(out[name].dtype))
    for name, factor in factors.items():
        out[name] = (out[name] * factor).astype(out[name].dtype)
    return out
```

```python
from contextlib import ExitStack

import numpy as np

import concourse.bass as bass
from concourse import mybir

F32 = mybir.dt.float32
I32 = mybir.dt.int32
U32 = mybir.dt.uint32
ALU = mybir.AluOpType
ACT = mybir.ActivationFunctionType
AX = mybir.AxisListType.X

P = 128
S = 256
T = S // P
D = 1024
KC = D // P
LAYERS = 2
EPS = 1e-6
MASKED = -1e30
BANK = 512

HEADS, KV_HEADS, HD = 8, 2, 64
QPK = HEADS // KV_HEADS
CMP_LEN, CMP_STRIDE, CMP_HID = 32, 16, 128
NCMP = (S - CMP_LEN) // CMP_STRIDE + 1
CONV_CH, TAPS = 512, 31
CC = CONV_CH // P
Q0, KCMP0, VCMP0, KSLC0, VSLC0, KWIN0, VWIN0, GATE0, GLU_A0, GLU_G0 = (
    0, 512, 640, 768, 896, 1024, 1152, 1280, 1304, 1816)
IN1 = 2328
F1 = 3584
J1 = F1 // 512
EXPERTS = 8
SLOTS = P

MLA_H, NOPE, MROPE, MLA_V, QR, KVR = 6, 64, 32, 64, 256, 128
DIFF_H, DIFF_D = 6, 32
MOBA_H = 4
CROSS_H, CROSS_D = 4, 256
CKV0, KR0, DQ0, DK0, DV0, MQ0, MK0, MV0 = 256, 384, 416, 800, 1184, 1568, 1824, 2080
IN2 = 2336
J2 = 4096 // 512
SLOPES = [2.0 ** (-8.0 * (h + 1) / (DIFF_H + MOBA_H)) for h in range(DIFF_H + MOBA_H)]

RING = 7
SLOTW = 4096

C1 = dict(attn=0, ffn=8, cb=16, lng=20, lnb=24, cw=28)
C1W = 28 + CC * TAPS
C2 = dict(attn=0, cross=8, mem=16, mlp=24, qn=32, kvn=34)
C2W = 35
B1W = 4 * HD
B2W = HD + 4 * DIFF_D


class Count:

    def __init__(self):
        self.block = self.lin = self.turn = self.norm = self.pow = 0
        self.unit = self.pt = self.hid = self.down = self.misc = 0


def build(nc, a, out):
    ctx = ExitStack()
    with ctx:
        def sb(name, shape, dt=F32):
            return ctx.enter_context(nc.sbuf_tensor(name, shape, dt))

        def sem(name):
            return ctx.enter_context(nc.semaphore(name))

        PS = ctx.enter_context(nc.psum_tensor("PS", [P, 8, BANK], F32))

        ring = sb("ring", [P, RING, SLOTW])
        X = sb("X", [P, T, D])
        H = sb("H", [P, T, D])
        HT = sb("HT", [P, KC, S])
        proj = sb("proj", [P, T, IN2])
        scr = sb("scr", [P, 6656])
        SM = sb("SM", [P, 2, 4, S])
        PT = sb("PT", [P, 2, 2, 4, P])
        ident = sb("ident", [P, P])
        ones = sb("ones", [P, P])
        mean_w = sb("mean_w", [P, P])
        before = sb("before", [P, P])
        slot_no = sb("slot_no", [P, P])
        causal = sb("causal", [P, S])
        cmask = sb("cmask", [P, T, 16])
        cvalid = sb("cvalid", [P, T])
        dist = sb("dist", [P, T, S])
        mhalf = sb("mhalf", [P, 1])
        cols = sb("cols", [P, 2 * C1W + 2 * C2W + EXPERTS * KC])
        bc = sb("bc", [P, 2 * B1W + 2 * B2W])
        cpos = sb("cpos", [HD, LAYERS, 2, CMP_LEN])
        cw2 = sb("cw2", [P, LAYERS, 2, HD])
        posi = sb("posi", [P, 8], I32)
        posf = sb("posf", [P, 8])
        rowi = sb("rowi", [P, S], I32)
        inv = sb("inv", [P, 24])
        ang = sb("ang", [P, 56])
        red = sb("red", [P, 2, 56])
        trig = sb("trig", [P, 2, 56])
        st = sb("st", [P, 48])
        lnv = sb("lnv", [P, S])
        rs = sb("rs", [P, S])
        rt = sb("rt", [P, 4, 192])
        mx = sb("mx", [P, 2, 4])
        nb = sb("nb", [P, 2, 4])
        sums = sb("sums", [P, 4, 4])
        coef = sb("coef", [P, 2, 4])
        otmp = sb("otmp", [P, 4 * HD])
        hid = sb("hid", [P, 2, 30])
        kc_sb = sb("kc_sb", [16, 4, HD])
        kcT = sb("kcT", [HD, 2, 16])
        lam = sb("lam", [P, 4])
        lam4 = sb("lam4", [P, 4])
        nit = sb("nit", [P, 2], I32)
        rt8 = sb("rt8", [P, 16, 16])
        idx8 = sb("idx8", [P, T, 8], U32)
        rk = sb("rk", [P, T, 16])
        g16 = sb("g16", [P, T, 16])

        QT = scr[:, 0:24 * S].rearrange("p (m s) -> p m s", s=S)
        CT = scr[:, 4096:4096 + CC * (S + TAPS - 1)].rearrange("p (c s) -> p c s", c=CC)
        Y = scr[:, 5248:5248 + CC * S].rearrange("p (c s) -> p c s", c=CC)
        SQ = scr[:, 4096:4096 + CC * S].rearrange("p (c s) -> p c s", c=CC)
        kblk = PT[:].rearrange("p a b c d -> p (a b c d)")[0:HD, 0:2 * CMP_LEN * 30].rearrange(
            "p (v l n) -> p v l n", v=2, l=CMP_LEN)
        HTf = HT[:].rearrange("p k s -> p (k s)")
        QM = HTf[:, 0:T * MLA_H * 96].rearrange("p (t h d) -> p t h d", t=T, h=MLA_H)
        CQT = HTf[:, 1152:1152 + 3 * S].rearrange("p (k s) -> p k s", s=S)
        KVH = scr[:, 19 * S:19 * S + T * MLA_H * P].rearrange("p (t n) -> p t n", t=T)
        MEM = scr[:, 0:T * D].rearrange("p (t d) -> p t d", t=T)
        CQ = MEM
        CQT8 = scr[:, 2048:4096].rearrange("p (k s) -> p k s", s=S)
        CKT8 = scr[:, 4096:6144].rearrange("p (k s) -> p k s", s=S)
        projf = proj[:].rearrange("p t n -> p (t n)")
        sil = projf[:, 0:1024].rearrange("p (t n) -> p t n", t=T)
        hm = projf[:, 1024:2048].rearrange("p (t n) -> p t n", t=T)
        hTf = projf[:, 2048:4096].rearrange("p (b k s) -> p b k s", b=2, k=4)
        xgT = scr[:, 0:1024].rearrange("p (k s) -> p k s", k=KC)
        disp = scr[:, 1024:1280].rearrange("p (t s) -> p t s", t=T)
        dispT = scr[:, 1280:1536].rearrange("p (t s) -> p t s", t=T)
        ye = scr[:, 1536:2560]
        hmT = scr[:, 2560:3584].rearrange("p (b k s) -> p b k s", b=2, k=4)

        const_ld = sem("const_ld")
        x_ld = sem("x_ld")
        const_ok = sem("const_ok")
        w_ld = [sem(f"w_ld{s}") for s in range(RING)]
        lin_full = sem("lin_full")
        lin_out = sem("lin_out")
        turned = sem("turned")
        turn_out = sem("turn_out")
        pow_in = sem("pow_in")
        pow_out = sem("pow_out")
        norm_rows = sem("norm_rows")
        norm_tr = sem("norm_tr")
        norm_T = sem("norm_T")
        sc_full = sem("sc_full")
        sm_ready = sem("sm_ready")
        p_ready = sem("p_ready")
        pt_full = sem("pt_full")
        pt_out = sem("pt_out")
        o_full = sem("o_full")
        o_out = sem("o_out")
        hid_full = sem("hid_full")
        hid_act = sem("hid_act")
        hid_rows = sem("hid_rows")
        hid_tr = sem("hid_tr")
        hid_T = sem("hid_T")
        down_done = sem("down_done")
        rows_ready = sem("rows_ready")
        conv_step = sem("conv_step")
        blk_ready = sem("blk_ready")
        ln_sq = sem("ln_sq")
        ln_ok = sem("ln_ok")
        ln_fin = sem("ln_fin")
        mixT_ok = sem("mixT_ok")
        lam_in = sem("lam_in")
        lam_ok = sem("lam_ok")
        trig_in = sem("trig_in")
        trig_ok = sem("trig_ok")
        mem_ld = sem("mem_ld")
        fin_ld = sem("fin_ld")
        x_done = sem("x_done")
        gate_in = sem("gate_in")
        gate_ok = sem("gate_ok")
        routed = sem("routed")
        router_a = sem("router_a")
        e_disp = sem("e_disp")
        e_gath = sem("e_gath")
        e_xg = sem("e_xg")
        e_dt = sem("e_dt")
        e_dts = sem("e_dts")
        e_gu = sem("e_gu")
        e_act = sem("e_act")
        e_rows = sem("e_rows")
        e_tr = sem("e_tr")
        e_T = sem("e_T")
        e_down = sem("e_down")
        e_y = sem("e_y")
        e_comb = sem("e_comb")
        e_acc = sem("e_acc")
        act_seq = sem("act_seq")
        dve_seq = sem("dve_seq")
        pool_seq = sem("pool_seq")
        out_st = sem("out_st")

        def col1(layer, name, n=1, off=0):
            c = layer * C1W + C1[name] + off
            return cols[:, c:c + n]

        def col2(layer, name, n=1, off=0):
            c = 2 * C1W + layer * C2W + C2[name] + off
            return cols[:, c:c + n]

        router_w = cols[:, 2 * (C1W + C2W):].rearrange("p (k e) -> p k e", e=EXPERTS)

        def slot(b, k, n, rows=P):
            return ring[0:rows, b % RING, 0:k * n].rearrange("p (k n) -> p k n", k=k)

        def bc4(ap, n):
            return ap.unsqueeze(2).to_broadcast([ap.shape[0], ap.shape[1], n])

        def unit(t, kl, scores, bias, scale, values, dv, end, kbs=None):
            return dict(t=t, kl=kl, scores=scores, bias=bias, scale=scale, values=values, dv=dv,
                        end=end, kbs=kbs or [P] * (kl // P))

        def tok(t):
            return slice(t * P, t * P + P)

        def nsa_units():
            out_ = []
            for br in range(3):
                for g in range(KV_HEADS):
                    for t in range(T):
                        heads = range(g * QPK, g * QPK + QPK)
                        if br == 0:
                            kl = NCMP
                            sc = [[(QT[0:HD, h, tok(t)], kcT[:, g, 0:NCMP])] for h in heads]
                            val = [[kc_sb[0:NCMP, 2 + g, :]] for _ in heads]
                            bias = ("shared", cmask[:, t, 0:NCMP])
                            kbs = [NCMP]
                        else:
                            kl = (t + 1) * P
                            kslot = (8 if br == 1 else 10) + g
                            v0 = (VSLC0 if br == 1 else VWIN0) + g * HD
                            sc = [[(QT[0:HD, h, tok(t)], QT[0:HD, kslot, 0:kl])] for h in heads]
                            val = [[proj[:, kb, v0:v0 + HD] for kb in range(t + 1)] for _ in heads]
                            bias = ("shared", causal[:, S - kl:])
                            kbs = None
                        out_.append(unit(t, kl, sc, bias, HD ** -0.5, val, HD, ("nsa", br, g), kbs))
            return out_

        def mla_units():
            out_ = []
            for h0, n in ((0, 4), (4, 2)):
                for t in range(T):
                    kl = (t + 1) * P
                    hs = range(h0, h0 + n)
                    sc = [[(QT[0:NOPE, h, tok(t)], QT[0:NOPE, 12 + h, 0:kl]),
                           (QT[0:MROPE, 6 + h, tok(t)], QT[0:MROPE, 18, 0:kl])] for h in hs]
                    val = [[KVH[:, kb, h * P + NOPE:h * P + P] for kb in range(t + 1)] for h in hs]
                    out_.append(unit(t, kl, sc, ("shared", causal[:, S - kl:]), 96 ** -0.5, val, MLA_V,
                                     ("plain", h0 * MLA_V)))
            return out_

        def diff_units():
            out_ = []
            for g in range(3):
                for t in range(T):
                    kl = (t + 1) * P
                    ms = range(4 * g, 4 * g + 4)
                    sc = [[(QT[0:DIFF_D, m, tok(t)], QT[0:DIFF_D, 12 + m, 0:kl])] for m in ms]
                    val = [[proj[:, kb, DV0 + (m // 2) * 64:DV0 + (m // 2) * 64 + 64]
                            for kb in range(t + 1)] for m in ms]
                    scale = DIFF_D ** -0.5
                    bias = ("slopes", dist[:, t, 0:kl], [-SLOPES[m // 2] / scale for m in ms])
                    out_.append(unit(t, kl, sc, bias, scale, val, 64, ("diff", 384 + g * 128)))
            return out_

        def moba_units():
            out_ = []
            for t in range(T):
                kl = (t + 1) * P
                sc = [[(QT[0:64, m, tok(t)], QT[0:64, 4 + m, 0:kl])] for m in range(MOBA_H)]
                val = [[proj[:, kb, MV0 + m * 64:MV0 + m * 64 + 64] for kb in range(t + 1)]
                       for m in range(MOBA_H)]
                scale = 64 ** -0.5
                bias = ("slopes", dist[:, t, 0:kl], [-SLOPES[DIFF_H + m] / scale for m in range(MOBA_H)])
                out_.append(unit(t, kl, sc, bias, scale, val, 64, ("plain", 768)))
            return out_

        def cross_units():
            out_ = []
            for g in range(2):
                for t in range(T):
                    hs = (2 * g, 2 * g + 1)
                    sc = [[(CQT8[:, 2 * h + c, tok(t)], CKT8[:, 2 * h + c, :]) for c in range(2)] for h in hs]
                    val = [[proj[:, kb, D + h * CROSS_D:D + (h + 1) * CROSS_D] for kb in range(2)] for h in hs]
                    out_.append(unit(t, S, sc, None, CROSS_D ** -0.5, val, CROSS_D,
                                     ("plain", 2 * g * CROSS_D)))
            return out_

        def heads_batch(src, base, width, n_heads, dst0, dst=None):
            out_ = []
            for h in range(0, n_heads, 2):
                k = min(2, n_heads - h)
                srcs = [src[:, t, base + (h + i) * width:base + (h + i + 1) * width]
                        for i in range(k) for t in range(T)]
                target = QT if dst is None else dst
                out_.append((srcs, target[0:width, dst0 + h:dst0 + h + k, :], None))
            return out_

        QMf = QM.rearrange("p t h d -> p t (h d)")
        t_conv = []
        for c in range(0, CC, 2):
            t_conv.append(([proj[:, t, GLU_A0 + (c + i) * P:GLU_A0 + (c + i + 1) * P]
                            for i in range(2) for t in range(T)],
                           CT[:, c:c + 2, TAPS - 1:TAPS - 1 + S], None))
        t_cmp = heads_batch(proj, KCMP0, HD, 4, 12)
        t_nsa = (heads_batch(proj, Q0, HD, 8, 0) + heads_batch(proj, KSLC0, HD, 2, 8)
                 + heads_batch(proj, KWIN0, HD, 2, 10))
        t_kc = [([kc_sb[0:NCMP, g, :] for g in range(2)], kcT[:, :, 0:NCMP], None)]
        t_mix1 = heads_batch(H, 0, P, 4, 0, HT)
        t_mix2 = heads_batch(H, 0, P, 8, 0, HT)
        t_cross = heads_batch(CQ, 0, P, 8, 0, CQT8) + heads_batch(proj, 0, P, 8, 0, CKT8)
        t_mla = []
        for src, base, width, step, n, dst0 in ((QMf, 0, NOPE, 96, 6, 0), (QMf, NOPE, MROPE, 96, 6, 6),
                                                (KVH, 0, NOPE, P, 6, 12), (proj, KR0, MROPE, 0, 1, 18)):
            for h in range(0, n, 2):
                k = min(2, n - h)
                t_mla.append(([src[:, t, base + (h + i) * step:base + (h + i) * step + width]
                               for i in range(k) for t in range(T)], QT[0:width, dst0 + h:dst0 + h + k, :], None))
        t_diff = heads_batch(proj, DQ0, DIFF_D, 12, 0) + heads_batch(proj, DK0, DIFF_D, 12, 12)
        t_moba = heads_batch(proj, MQ0, 64, 4, 0) + heads_batch(proj, MK0, 64, 4, 4)

        def t_latent(layer):
            return [([proj[:, t, k * P:k * P + P] for t in range(T)], CQT[:, k:k + 1, :],
                     col2(layer, "qn", 1, k) if k < 2 else col2(layer, "kvn")) for k in range(3)]

        IN1_BLOCKS = [(GLU_A0, 512), (GLU_G0, 512), (0, 512), (512, 512), (1024, 280)]
        IN2_BLOCKS = [(0, 416), (416, 512), (928, 512), (1440, 512), (1952, 384)]

        block = ctx.enter_context(nc.Block())

        @block.sync
        def _(sp):
            c = Count()
            users = []

            def load(src, k, n, rows=P, view=None):
                b = len(users)
                if b >= RING:
                    sp.wait_ge(*users[b - RING])
                dst = slot(b, k, n, rows)
                sp.dma_start(dst, src).then_inc(w_ld[b % RING], 16)

            def rows_of(w, k0, k, c0, n):
                return w[k0:k0 + k * P, c0:c0 + n].rearrange("(k p) n -> p k n", p=P)

            def lin_block(src, k, n, outs, rows=P):
                load(src, k, n, rows)
                c.lin += outs
                users.append((lin_full, c.lin))

            def ffn(ws, wd, chunks):
                for j in range(chunks):
                    for w in ws:
                        load(rows_of(w, 0, KC, j * 512, 512), KC, 512)
                        users.append((hid_full, c.hid + 2 * (j + 1)))
                    load(rows_of(wd, j * 512, 4, 0, D), 4, D)
                    users.append((down_done, c.down + j + 1))
                c.hid += 2 * chunks
                c.down += chunks

            sp.dma_start(X[:], a["x"].rearrange("b (t p) d -> p (b t) d", p=P)).then_inc(x_ld, 16)
            sp.dma_start(cols[:], a["cols"]).then_inc(const_ld, 16)
            sp.dma_start(bc[:], a["bc"].to_broadcast([P, a["bc"].shape[1]])).then_inc(const_ld, 16)
            sp.dma_start(cpos[:], a["cpos"]).then_inc(const_ld, 16)
            sp.dma_start(cw2[:], a["cw2"]).then_inc(const_ld, 16)
            sp.dma_start(posi[:, 0:5], a["posc"]).then_inc(const_ld, 16)
            sp.dma_start(rowi[:], a["positions_2"].to_broadcast([P, S])).then_inc(const_ld, 16)

            for layer in range(LAYERS):
                w = a["w_in"][layer]
                for c0, n in IN1_BLOCKS:
                    lin_block(rows_of(w, 0, KC, c0, n), KC, n, T)
                for name in ("cmp_w1_k", "cmp_w1_v"):
                    lin_block(a[name][layer].rearrange("(l d) h -> d l h", d=HD), CMP_LEN, CMP_HID, 1, HD)
                c.lin += 1
                c.lin += 2
                for n in range(2):
                    lin_block(rows_of(a["w_out"][layer], 0, KC, n * 512, 512), KC, 512, T)
                if layer == 0:
                    ffn([a["ffn_w_gate"][0], a["ffn_w_up"][0]], a["ffn_w_down"][0], J1)
                    continue
                base = len(users)
                c.lin += 2

                def moe_src(e, i):
                    j, kind = divmod(i, 3)
                    if kind < 2:
                        w3 = a["moe_w_gate"] if kind == 0 else a["moe_w_up"]
                        return w3[0].rearrange("e d f -> (e d) f")[
                            bass.ds(e * D, D), j * 512:j * 512 + 512].rearrange("(k p) f -> p k f", p=P)
                    return a["moe_w_down"][0].rearrange("e f d -> (e f) d")[
                        bass.ds(e * F1 + j * 512, 512), :].rearrange("(k p) f -> p k f", p=P)

                def moe_dst(i):
                    return slot(base + i, KC, 512) if i % 3 < 2 else slot(base + i, 4, D)

                NB = 3 * J1
                for i in range(RING):
                    sp.wait_ge(*users[base + i - RING])
                    sp.dma_start(moe_dst(i), moe_src(0, i)).then_inc(w_ld[(base + i) % RING], 16)
                sp.wait_ge(routed, 1)
                last = sp.value_load(nit[0:1, 1:2], min_val=EXPERTS - 1, max_val=2 * EXPERTS - 1)
                with sp.Fori(0, last) as it:
                    e0 = sp.snap(it & 7)
                    e1 = sp.snap((it + 1) & 7)
                    for e, i in ((e0, 0), (e0, 2), (e1, 0), (e1, 2)):
                        sp.lower_ap_dma(moe_src(e, i))
                    free = [sp.snap(it * J1 + (j + 1)) for j in range(J1)]
                    for f in free:
                        sp.to_reg(f)
                    for i in range(RING, NB + RING):
                        jj, kind = divmod(i - RING, 3)
                        sp.wait_ge(e_gu if kind < 2 else e_down, free[jj])
                        sp.dma_start(moe_dst(i), moe_src(e0 if i < NB else e1, i % NB)).then_inc(
                            w_ld[(base + i) % RING], 16)
                free = [sp.snap(last * J1 + (j + 1)) for j in range(J1)]
                for f in free:
                    sp.to_reg(f)
                for i in range(RING, NB):
                    jj, kind = divmod(i - RING, 3)
                    sp.wait_ge(e_gu if kind < 2 else e_down, free[jj])
                    sp.dma_start(moe_dst(i), moe_src(EXPERTS - 1, i)).then_inc(w_ld[(base + i) % RING], 16)
                for i in range(NB - RING, NB):
                    jj, kind = divmod(i, 3)
                    users.append((e_gu if kind < 2 else e_down, free[jj]))
                assert NB % RING == 0

            for layer in range(LAYERS):
                w = a["w_in_2"][layer]
                for c0, n in IN2_BLOCKS:
                    lin_block(rows_of(w, 0, KC, c0, n), KC, n, T)
                lin_block(rows_of(a["mla_w_uq_2"][layer], 0, 2, 0, 576), 2, 576, 2 * T)
                lin_block(rows_of(a["mla_w_ukv_2"][layer], 0, 1, 0, 768), 1, 768, 2 * T)
                c.unit += 12
                sp.wait_ge(o_full, 24 + c.unit)
                sp.dma_start(MEM, a["mem_2"].rearrange("b (t p) d -> p (b t) d", p=P)).then_inc(mem_ld, 16)
                c.unit += 4
                for n in range(2):
                    lin_block(rows_of(a["w_out_2"][layer], 0, KC, n * 512, 512), KC, 512, T)
                for n in range(4):
                    lin_block(rows_of(a["cross_wkv_2"][layer], 0, KC, n * 512, 512), KC, 512, T)
                for n in range(2):
                    lin_block(rows_of(a["cross_wq_2"][layer], 0, KC, n * 512, 512), KC, 512, T)
                for n in range(2):
                    lin_block(rows_of(a["cross_wo_2"][layer], 0, KC, n * 512, 512), KC, 512, T)
                ffn([a["mlp_w1_2"][layer]], a["mlp_w2_2"][layer], J2)
            sp.wait_ge(o_full, 24 + c.unit)
            sp.dma_start(MEM[:, 0, :], a["final_norm_2"].to_broadcast([P, D])).then_inc(fin_ld, 16)
            sp.wait_ge(x_done, 1)
            sp.dma_start(out.rearrange("b (t p) d -> p (b t) d", p=P), H[:]).then_inc(out_st, 16)
            sp.wait_ge(out_st, 16)

        @block.gpsimd
        def _(pool):
            c = Count()

            def power(n):
                for _ in range(n):
                    c.pow += 1
                    pool.wait_ge(pow_in, c.pow)
                    pool.tensor_tensor(rs[:, 0:48], st[:, 0:48], mhalf[:].to_broadcast([P, 48]),
                                       ALU.pow).then_inc(pow_out, 1)

            n = 0
            for tile, v in ((ident, 0.0), (ones, 1.0), (mean_w, 1.0 / CONV_CH), (before, 1.0),
                            (causal, 0.0), (cmask, 0.0), (cvalid, 1.0), (mhalf, -0.5), (st, 1.0), (ang, 0.0),
                            (posf, 0.0), (kc_sb, 0.0)):
                pool.memset(tile[:], v).then_inc(pool_seq, 1)
                n += 1
            half1 = np.float32(500000.0) ** (-2.0 * np.arange(8, dtype=np.float32) / np.float32(16))
            half2 = np.float32(10000.0) ** (-np.arange(16, dtype=np.float32) / np.float32(16))
            for i, v in enumerate(list(half1) + list(half2)):
                pool.memset(inv[:, i:i + 1], float(np.float32(v))).then_inc(pool_seq, 1)
                n += 1
            pool.wait_ge(pool_seq, n)
            pool.affine_select(out=ident[:], in_=ident[:], compare_op=ALU.not_equal, fill=1.0, base=0,
                               pattern=[[-1, P]], channel_multiplier=1).then_inc(const_ok, 1)
            pool.affine_select(out=before[:], in_=before[:], compare_op=ALU.is_gt, fill=0.0, base=0,
                               pattern=[[1, P]], channel_multiplier=-1).then_inc(const_ok, 1)
            pool.affine_select(out=causal[:, P:S], in_=causal[:, P:S], compare_op=ALU.is_ge, fill=MASKED,
                               base=0, pattern=[[-1, P]], channel_multiplier=1).then_inc(const_ok, 1)
            for t in range(T):
                pool.affine_select(out=cmask[:, t, :], in_=cmask[:, t, :], compare_op=ALU.is_ge, fill=MASKED,
                                   base=t * P - (CMP_LEN - 1), pattern=[[-CMP_STRIDE, 16]],
                                   channel_multiplier=1).then_inc(const_ok, 1)
            pool.affine_select(out=cvalid[:, 0:1], in_=cvalid[:, 0:1], compare_op=ALU.is_ge, fill=0.0,
                               base=-(CMP_LEN - 1), pattern=[[0, 1]], channel_multiplier=1).then_inc(const_ok, 1)
            pool.iota(slot_no[:], pattern=[[1, P]], base=0, channel_multiplier=0,
                      allow_small_or_imprecise_dtypes=True).then_inc(const_ok, 1)
            for layer in range(LAYERS):
                power(3)
                pool.wait_ge(lin_out, 19 * layer + 15)
                pool.tensor_tensor(rs[:], lnv[:], mhalf[:].to_broadcast([P, S]), ALU.pow).then_inc(ln_ok, 1)
                power(1)
            for layer in range(LAYERS):
                power(6)
            power(1)
        CONST_OK = 7

        @block.tensor
        def _(pe):
            c = Count()
            used = [0] * RING

            def wait_block():
                s = c.block % RING
                used[s] += 1
                pe.wait_ge(w_ld[s], 16 * used[s])
                c.block += 1
                return c.block - 1

            def lin_bank():
                if c.lin >= 4:
                    pe.wait_ge(lin_out, c.lin - 3)
                c.lin += 1
                return 4 + (c.lin - 1) % 4

            def linear(lhs, k, n_all, n):
                b = wait_block()
                w = slot(b, k, n_all)
                for c0 in range(0, n_all, n):
                    for t in range(T):
                        bank = lin_bank()
                        for kc in range(k):
                            mm = pe.matmul(PS[:, bank, 0:n], lhs(kc, t), w[:, kc, c0:c0 + n],
                                           start=(kc == 0), stop=(kc == k - 1))
                        mm.then_inc(lin_full, 1)

            def turn(batches):
                for srcs, dst, gain in batches:
                    if c.turn >= 4:
                        pe.wait_ge(turn_out, c.turn - 3)
                    off = 0
                    for s in srcs:
                        rows, width = s.shape[0], s.shape[1]
                        mm = pe.transpose(PS[0:width, c.turn % 4, off:off + rows], s, ident[0:rows, 0:rows])
                        off += rows
                    mm.then_inc(turned, 1)
                    c.turn += 1

            def norm():
                for b in range(4):
                    t, half = divmod(b, 2)
                    pe.wait_ge(norm_rows, 2 * c.norm + t + 1)
                    for i in range(4):
                        kc = half * 4 + i
                        mm = pe.transpose(PS[:, b, i * P:i * P + P], H[:, t, kc * P:kc * P + P], ident[:])
                    mm.then_inc(norm_tr, 1)
                c.norm += 1
                pe.wait_ge(norm_T, 4 * c.norm)

            def rows(n=1):
                c.misc += n
                pe.wait_ge(rows_ready, c.misc)

            def attention(units):
                pe.wait_ge(lin_out, c.lin)
                pe.wait_ge(turn_out, c.turn)
                u0 = c.unit
                xs = [c.pt]
                for un in units:
                    xs.append(xs[-1] + len(un["kbs"]))

                def scores(i):
                    u, un = u0 + i, units[i]
                    if u >= 2:
                        pe.wait_ge(sm_ready, u - 1)
                    for m, pairs in enumerate(un["scores"]):
                        for k, (q, key) in enumerate(pairs):
                            mm = pe.matmul(PS[:, 2 * (u % 2) + m // 2, (m % 2) * S:(m % 2) * S + un["kl"]],
                                           q, key, start=(k == 0), stop=(k == len(pairs) - 1))
                    mm.then_inc(sc_full, 1)

                def probs(i):
                    u, un = u0 + i, units[i]
                    pe.wait_ge(p_ready, u + 1)
                    for kb, size in enumerate(un["kbs"]):
                        x = xs[i] + kb
                        if x >= 2:
                            pe.wait_ge(pt_out, x - 1)
                        for m in range(len(un["scores"])):
                            mm = pe.transpose(PS[0:size, 4 + x % 2, m * P:m * P + P],
                                              SM[:, u % 2, m, kb * P:kb * P + size], ident[:])
                        mm.then_inc(pt_full, 1)

                def values(i):
                    u, un = u0 + i, units[i]
                    pe.wait_ge(pt_out, xs[i + 1])
                    if u >= 2:
                        pe.wait_ge(o_out, u - 1)
                    dv = un["dv"]
                    for m, vs in enumerate(un["values"]):
                        for kb, v in enumerate(vs):
                            mm = pe.matmul(PS[:, 6 + u % 2, m * dv:(m + 1) * dv],
                                           PT[0:un["kbs"][kb], u % 2, kb, m, :], v,
                                           start=(kb == 0), stop=(kb == len(vs) - 1))
                    mm.then_inc(o_full, 1)

                for i in range(len(units) + 2):
                    if i < len(units):
                        scores(i)
                    if 1 <= i <= len(units):
                        probs(i - 1)
                    if i >= 2:
                        values(i - 2)
                c.unit += len(units)
                c.pt = xs[-1]
                pe.wait_ge(o_out, c.unit)

            def ffn(chunks, gated):
                def hidden(j, t):
                    for g in range(2 if gated else 1):
                        bank = 2 * t + g if gated else 2 * t + j % 2
                        for kc in range(KC):
                            mm = pe.matmul(PS[:, bank, :], HT[:, kc, tok(t)], blocks[g][:, kc, :],
                                           start=(kc == 0), stop=(kc == KC - 1))
                    mm.then_inc(hid_full, 1)

                def turn_hidden(j, t):
                    q = c.hid + 2 * j + t
                    pe.wait_ge(hid_rows, q + 1)
                    bank = 2 * t if gated else 2 * t + j % 2
                    for i in range(4):
                        mm = pe.transpose(PS[:, bank, i * P:i * P + P], hm[:, t, i * P:i * P + P], ident[:])
                    mm.then_inc(hid_tr, 1)

                def down(j, w):
                    for t in range(T):
                        pe.wait_ge(hid_T, c.hid + 2 * j + t + 1)
                        for i in range(4):
                            for half in range(2):
                                mm = pe.matmul(PS[:, 4 + 2 * t + half, :], hTf[:, j % 2, i, tok(t)],
                                               w[:, i, half * 512:half * 512 + 512],
                                               start=(j == 0 and i == 0), stop=(j == chunks - 1 and i == 3))
                    mm.then_inc(down_done, 1)

                wdown = None
                for j in range(chunks + 1):
                    if j < chunks:
                        blocks = [slot(wait_block(), KC, 512) for _ in range(2 if gated else 1)]
                        for t in range(T):
                            if j >= 1:
                                pe.wait_ge(hid_T, c.hid + 2 * (j - 1) + t + 1)
                            hidden(j, t)
                        turn_hidden(j, 0)
                    if j >= 1:
                        down(j - 1, wdown)
                    if j < chunks:
                        turn_hidden(j, 1)
                        wdown = slot(wait_block(), 4, D)
                c.hid += 2 * chunks
                c.down += chunks
                pe.wait_ge(hid_T, c.hid)

            def moe():
                bank = lin_bank()
                for t in range(T):
                    for kc in range(KC):
                        mm = pe.matmul(PS[:, bank, t * 8:t * 8 + 8], HT[:, kc, tok(t)], router_w[:, kc, :],
                                       start=(kc == 0), stop=(kc == KC - 1))
                mm.then_inc(lin_full, 1)
                bank = lin_bank()
                pe.wait_ge(router_a, 1)
                asg = [rt8[:, t, 0:8] for t in range(T)]
                for col, pairs in ((0, [(before, 0)]), (8, [(ones, 0), (before, 1)]), (16, [(ones, 0), (ones, 1)])):
                    for k, (m_, t) in enumerate(pairs):
                        mm = pe.matmul(PS[:, bank, col:col + 8], m_[:], asg[t], start=(k == 0),
                                       stop=(k == len(pairs) - 1))
                mm.then_inc(lin_full, 1)
                base = c.block
                pe.wait_ge(routed, 1)
                steps = pe.value_load(nit[0:1, 0:1], min_val=EXPERTS, max_val=2 * EXPERTS)

                def arrived(it, i):
                    s = (base + i) % RING
                    per = 3 * J1 // RING
                    pe.wait_ge(w_ld[s], it * (16 * per) + 16 * (used[s] + i // RING + 1))
                    return base + i

                with pe.Fori(0, steps) as it:
                    pe.wait_ge(e_disp, it + 1)
                    for k in range(KC):
                        for t in range(T):
                            mm = pe.matmul(PS[:, 6 + k // 4, (k % 4) * P:(k % 4) * P + P],
                                           H[:, t, k * P:k * P + P], disp[:, t, :], start=(t == 0), stop=(t == T - 1))
                        if k % 4 == 3:
                            mm.then_inc(e_gath, 1)
                    for t in range(T):
                        mm = pe.transpose(PS[:, 5, t * P:t * P + P], disp[:, t, :], ident[:])
                    mm.then_inc(e_dt, 1)
                    pe.wait_ge(e_xg, it * 2 + 2)
                    pe.wait_ge(e_dts, it + 1)

                    def gate_up(j):
                        for g in range(2):
                            w = slot(arrived(it, 3 * j + g), KC, 512)
                            if g == 0 and j >= 2:
                                pe.wait_ge(e_T, it * J1 + (j - 1))
                            for kc in range(KC):
                                mm = pe.matmul(PS[:, 2 * (j % 2) + g, :], xgT[:, kc, :], w[:, kc, :],
                                               start=(kc == 0), stop=(kc == KC - 1))
                        mm.then_inc(e_gu, 1)

                    def turn_rows(j):
                        pe.wait_ge(e_rows, it * J1 + (j + 1))
                        for i in range(4):
                            mm = pe.transpose(PS[:, 2 * (j % 2), i * P:i * P + P], hm[:, j % 2, i * P:i * P + P],
                                              ident[:])
                        mm.then_inc(e_tr, 1)

                    def down(j):
                        w = slot(arrived(it, 3 * j + 2), 4, D)
                        pe.wait_ge(e_T, it * J1 + (j + 1))
                        for i in range(4):
                            for half in range(2):
                                mm = pe.matmul(PS[:, 4 + half, :], hmT[:, j % 2, i, :],
                                               w[:, i, half * 512:half * 512 + 512],
                                               start=(j == 0 and i == 0), stop=(j == J1 - 1 and i == 3))
                        mm.then_inc(e_down, 1)

                    for j in range(J1 + 2):
                        if j < J1:
                            gate_up(j)
                        if 1 <= j <= J1:
                            turn_rows(j - 1)
                        if j >= 2:
                            down(j - 2)
                    pe.wait_ge(e_y, it * 2 + 2)
                    for t in range(T):
                        for half in range(2):
                            k = 2 * t + half
                            if k >= 2:
                                pe.wait_ge(e_acc, it * 4 + (k - 1))
                            pe.matmul(PS[:, 6 + k % 2, :], dispT[:, t, :], ye[:, half * 512:half * 512 + 512],
                                      start=True, stop=True).then_inc(e_comb, 1)
                    pe.wait_ge(e_acc, it * 4 + 4)
                return steps

            def ht(kc, t):
                return HT[:, kc, tok(t)]

            pe.wait_ge(const_ok, CONST_OK)
            pe.wait_ge(const_ld, 16 * 6)
            for layer in range(LAYERS):
                norm()
                for c0, n in IN1_BLOCKS[0:3]:
                    linear(ht, KC, n, n)
                rows()
                turn(t_conv)
                for c0, n in IN1_BLOCKS[3:]:
                    linear(ht, KC, n, n)
                pe.wait_ge(lin_out, c.lin)
                turn(t_cmp)
                for v in range(2):
                    w = slot(wait_block(), CMP_LEN, CMP_HID, HD)
                    bank = lin_bank()
                    pe.wait_ge(blk_ready, layer + 1)
                    for l in range(CMP_LEN):
                        mm = pe.matmul(PS[:, bank, 0:30], w[:, l, :], kblk[:, v, l, :], start=(l == 0),
                                       stop=(l == CMP_LEN - 1))
                    mm.then_inc(lin_full, 1)
                bank = lin_bank()
                pe.wait_ge(lin_out, c.lin - 1)
                for v in range(2):
                    for g in range(2):
                        mm = pe.matmul(PS[0:NCMP, bank, (2 * v + g) * HD:(2 * v + g + 1) * HD],
                                       hid[:, v, g * NCMP:(g + 1) * NCMP], cw2[:, layer, v, :], start=True, stop=True)
                mm.then_inc(lin_full, 1)
                rows()
                turn(t_nsa)
                rows()
                turn(t_kc)
                attention(nsa_units())
                for part in range(2):
                    bank = lin_bank()
                    if part == 0:
                        pe.wait_ge(conv_step, (layer + 1) * CC * TAPS)
                    else:
                        pe.wait_ge(ln_sq, layer + 1)
                    for k in range(CC):
                        mm = pe.matmul(PS[:, bank, 0:S], mean_w[:], (Y if part == 0 else SQ)[:, k, :],
                                       start=(k == 0), stop=(k == CC - 1))
                    mm.then_inc(lin_full, 1)
                turn(t_mix1)
                pe.wait_ge(turn_out, c.turn)
                pe.wait_ge(mixT_ok, layer + 1)
                for n in range(2):
                    linear(ht, KC, 512, 512)
                norm()
                if layer == 0:
                    ffn(J1, True)
                else:
                    steps = moe()
            per = 3 * J1 // RING
            extra = pe.snap(steps * (16 * per))

            def wait_block():
                s = c.block % RING
                used[s] += 1
                pe.wait_ge(w_ld[s], extra + 16 * used[s])
                c.block += 1
                return c.block - 1

            for layer in range(LAYERS):
                norm()
                for c0, n in IN2_BLOCKS:
                    linear(ht, KC, n, n)
                rows()
                turn(t_latent(layer))
                pe.wait_ge(turn_out, c.turn)
                linear(lambda kc, t: CQT[:, kc, tok(t)], 2, 576, 288)
                linear(lambda kc, t: CQT[:, 2, tok(t)], 1, 768, 384)
                pe.wait_ge(lin_out, c.lin)
                rows()
                turn(t_mla)
                attention(mla_units())
                turn(t_diff)
                attention(diff_units())
                turn(t_moba)
                attention(moba_units())
                rows()
                turn(t_mix2)
                pe.wait_ge(turn_out, c.turn)
                for n in range(2):
                    linear(ht, KC, 512, 512)
                norm()
                for n in range(4):
                    linear(ht, KC, 512, 512)
                norm()
                for n in range(2):
                    linear(ht, KC, 512, 512)
                pe.wait_ge(lin_out, c.lin)
                turn(t_cross)
                attention(cross_units())
                turn(t_mix2)
                pe.wait_ge(turn_out, c.turn)
                for n in range(2):
                    linear(ht, KC, 512, 512)
                norm()
                ffn(J2, False)

        @block.scalar
        def _(act):
            c = Count()

            def take(dst, func=ACT.Copy, n=None, rows=P, more=None):
                c.lin += 1
                act.wait_ge(lin_full, c.lin)
                bank = 4 + (c.lin - 1) % 4
                width = n or dst.shape[-1]
                if more:
                    d2, f2, o2 = more
                    act.activation(dst, PS[0:rows, bank, 0:width], func)
                    return act.activation(d2, PS[0:rows, bank, o2:o2 + d2.shape[-1]], f2).then_inc(lin_out, 1)
                return act.activation(dst, PS[0:rows, bank, 0:width], func).then_inc(lin_out, 1)

            def turn(batches):
                for srcs, dst, gain in batches:
                    act.wait_ge(turned, c.turn + 1)
                    width = srcs[0].shape[1]
                    n = sum(s.shape[0] for s in srcs)
                    src = PS[0:width, c.turn % 4, 0:n].rearrange("p (m s) -> p m s", m=dst.shape[1])
                    if gain is None:
                        act.activation(dst, src, ACT.Copy).then_inc(turn_out, 1)
                    else:
                        act.activation(dst, src, ACT.Copy, scale=gain).then_inc(turn_out, 1)
                    c.turn += 1

            def attention(units):
                u0 = c.unit
                xs = [c.pt]
                for un in units:
                    xs.append(xs[-1] + len(un["kbs"]))

                def exps(i):
                    u, un = u0 + i, units[i]
                    act.wait_ge(sm_ready, u + 1)
                    if u >= 4:
                        act.wait_ge(o_out, u - 3)
                    for m in range(len(un["scores"])):
                        row = SM[:, u % 2, m, 0:un["kl"]]
                        ins = act.activation(row, row, ACT.Exp, bias=nb[:, u % 2, m:m + 1], scale=un["scale"],
                                             accum_out=sums[:, u % 4, m:m + 1])
                    ins.then_inc(p_ready, 1)

                def copies(i):
                    u, un = u0 + i, units[i]
                    n = len(un["scores"])
                    for kb, size in enumerate(un["kbs"]):
                        x = xs[i] + kb
                        act.wait_ge(pt_full, x + 1)
                        if u >= 2:
                            act.wait_ge(o_full, u - 1)
                        act.activation(PT[0:size, u % 2, kb, 0:n, :],
                                       PS[0:size, 4 + x % 2, 0:n * P].rearrange("p (m s) -> p m s", m=n),
                                       ACT.Copy).then_inc(pt_out, 1)

                for i in range(len(units) + 1):
                    if i < len(units):
                        exps(i)
                    if i >= 1:
                        copies(i - 1)
                c.unit += len(units)
                c.pt = xs[-1]

            def ffn(chunks, gated):
                for j in range(chunks):
                    for t in range(T):
                        q = c.hid + 2 * j + t
                        act.wait_ge(hid_full, q + 1)
                        if q >= 2:
                            act.wait_ge(hid_rows, q - 1)
                        bank = 2 * t if gated else 2 * t + j % 2
                        act.activation(sil[:, t, :], PS[:, bank, :], ACT.Silu if gated else ACT.Relu).then_inc(
                            hid_act, 1)
                    for t in range(T):
                        q = c.hid + 2 * j + t
                        act.wait_ge(hid_tr, q + 1)
                        if j >= 2:
                            act.wait_ge(down_done, c.down + j - 1)
                        bank = 2 * t if gated else 2 * t + j % 2
                        act.activation(hTf[:, j % 2, :, tok(t)],
                                       PS[:, bank, :].rearrange("p (k s) -> p k s", k=4), ACT.Copy).then_inc(
                            hid_T, 1)
                c.hid += 2 * chunks
                c.down += chunks

            def moe():
                c.lin += 2
                act.wait_ge(gate_in, 1)
                act.activation(rt8[:, 8, 0:T], rt8[:, 7, 0:T], ACT.Exp).then_inc(gate_ok, 1)
                act.wait_ge(routed, 1)
                steps = act.value_load(nit[0:1, 0:1], min_val=EXPERTS, max_val=2 * EXPERTS)
                with act.Fori(0, steps) as it:
                    act.wait_ge(e_dt, it + 1)
                    act.activation(dispT[:].rearrange("p t s -> p (t s)"), PS[:, 5, 0:2 * P],
                                   ACT.Copy).then_inc(e_dts, 1)

                    def copy(j):
                        act.wait_ge(e_tr, it * J1 + (j + 1))
                        if j >= 2:
                            act.wait_ge(e_down, it * J1 + (j - 1))
                        act.activation(hmT[:, j % 2, :, :],
                                       PS[:, 2 * (j % 2), :].rearrange("p (k s) -> p k s", k=4),
                                       ACT.Copy).then_inc(e_T, 1)

                    for j in range(J1):
                        act.wait_ge(e_gu, it * J1 + (j + 1))
                        if j >= 2:
                            act.wait_ge(e_rows, it * J1 + (j - 1))
                        act.activation(sil[:, j % 2, :], PS[:, 2 * (j % 2), :], ACT.Silu).then_inc(e_act, 1)
                        if j >= 1:
                            copy(j - 1)
                    copy(J1 - 1)
                    act.wait_ge(e_down, it * J1 + J1)
                    for half in range(2):
                        act.activation(ye[:, half * 512:half * 512 + 512], PS[:, 4 + half, :],
                                       ACT.Copy).then_inc(e_y, 1)

            act.wait_ge(trig_in, 1)
            act.activation(trig[:].rearrange("p a b -> p (a b)"), red[:].rearrange("p a b -> p (a b)"),
                           ACT.Sin).then_inc(trig_ok, 1)
            for layer in range(LAYERS):
                for k, (c0, n) in enumerate(IN1_BLOCKS):
                    for t in range(T):
                        if k < 4:
                            take(proj[:, t, c0:c0 + n], ACT.Sigmoid if k == 1 else ACT.Copy)
                        else:
                            take(proj[:, t, c0:c0 + 256], more=(proj[:, t, GATE0:GATE0 + 24], ACT.Sigmoid, 256))
                    if k == 2:
                        turn(t_conv)
                turn(t_cmp)
                for v in range(2):
                    take(hid[:, v, :], ACT.Gelu_apprx_tanh)
                take(kc_sb[0:NCMP, :, :].rearrange("p a b -> p (a b)"), rows=NCMP)
                turn(t_nsa)
                turn(t_kc)
                attention(nsa_units())
                c.lin += 2
                turn(t_mix1)
                act.wait_ge(ln_fin, layer + 1)
                for k in range(CC):
                    ins = act.activation(HT[:, CC + k, :], Y[:, k, :], ACT.Silu, bias=col1(layer, "lnb", 1, k),
                                         scale=col1(layer, "lng", 1, k))
                ins.then_inc(mixT_ok, 1)
                c.lin += 4
                if layer == 0:
                    ffn(J1, True)
                else:
                    moe()
            for layer in range(LAYERS):
                for c0, n in IN2_BLOCKS:
                    for t in range(T):
                        take(proj[:, t, c0:c0 + n])
                act.wait_ge(lam_in, layer + 1)
                act.activation(lam[:, 0:2], lam[:, 0:2], ACT.Exp).then_inc(lam_ok, 1)
                turn(t_latent(layer))
                for half in range(2):
                    for t in range(T):
                        take(QMf[:, t, half * 288:half * 288 + 288])
                for half in range(2):
                    for t in range(T):
                        take(KVH[:, t, half * 384:half * 384 + 384])
                turn(t_mla)
                attention(mla_units())
                turn(t_diff)
                attention(diff_units())
                turn(t_moba)
                attention(moba_units())
                turn(t_mix2)
                c.lin += 4
                for n in range(4):
                    for t in range(T):
                        take(proj[:, t, n * 512:n * 512 + 512])
                for n in range(2):
                    for t in range(T):
                        take(CQ[:, t, n * 512:n * 512 + 512])
                turn(t_cross)
                attention(cross_units())
                turn(t_mix2)
                c.lin += 4
                ffn(J2, False)

        @block.vector
        def _(dve):
            c = Count()
            done = [0]

            def seq(ins):
                done[0] += 1
                ins.then_inc(dve_seq, 1)
                dve.wait_ge(dve_seq, done[0])

            def power():
                c.pow += 1
                dve.wait_ge(pow_out, c.pow)

            def mean_eps(n, width):
                dve.tensor_scalar(st[:, 0:n], st[:, 0:n], 1.0 / width, EPS, ALU.mult, ALU.add).then_inc(pow_in, 1)
                power()

            def norm(src, gains=None):
                for t in range(T):
                    seq(dve.tensor_tensor_reduce(H[:, t, :], src[:, t, :], src[:, t, :], 1.0, 0.0, ALU.mult,
                                                 ALU.add, st[:, t:t + 1]))
                mean_eps(T, D)
                for t in range(T):
                    dve.tensor_scalar(H[:, t, :], src[:, t, :], rs[:, t:t + 1], None, ALU.mult).then_inc(norm_rows, 1)
                if gains is not None:
                    for b in range(4):
                        t, half = divmod(b, 2)
                        dve.wait_ge(norm_tr, 4 * c.norm + b + 1)
                        dve.tensor_tensor(HT[:, half * 4:half * 4 + 4, tok(t)],
                                          PS[:, b, :].rearrange("p (k s) -> p k s", k=4),
                                          bc4(gains[:, half * 4:half * 4 + 4], P), ALU.mult).then_inc(norm_T, 1)
                    c.norm += 1

            def bank_of():
                c.lin += 1
                dve.wait_ge(lin_full, c.lin)
                return 4 + (c.lin - 1) % 4

            def add_out():
                for n in range(2):
                    for t in range(T):
                        bank = bank_of()
                        row = X[:, t, n * 512:n * 512 + 512]
                        dve.tensor_tensor(row, PS[:, bank, :], row, ALU.add).then_inc(lin_out, 1)
                dve.wait_ge(lin_out, c.lin)

            def heads_norm(src, s0, n, width, gain, rs0):
                seq(dve.tensor_tensor(src, src, bc4(rs[:, rs0:rs0 + n][0:src.shape[0]], width), ALU.mult))
                seq(dve.tensor_tensor(src, src, gain.unsqueeze(1).to_broadcast([src.shape[0], n, width]), ALU.mult))

            def rotate(x1, x2, cos, sin, n, half, signal=None):
                p = x1.shape[0]
                r = [rt[0:p, i, 0:n * half].rearrange("p (n h) -> p n h", n=n) for i in range(4)]
                cb = cos.unsqueeze(1).to_broadcast([p, n, half])
                sb_ = sin.unsqueeze(1).to_broadcast([p, n, half])
                dve.tensor_tensor(r[0], x1, cb, ALU.mult)
                dve.tensor_tensor(r[1], x2, sb_, ALU.mult)
                dve.tensor_tensor(r[2], x2, cb, ALU.mult)
                seq(dve.tensor_tensor(r[3], x1, sb_, ALU.mult))
                dve.tensor_tensor(x1, r[0], r[1], ALU.subtract)
                last = dve.tensor_tensor(x2, r[2], r[3], ALU.add)
                if signal is None:
                    seq(last)
                else:
                    last.then_inc(signal, 1)

            def conv_ops(layer, k0, k1):
                for k in range(k0, k1):
                    j, ch = divmod(k, CC)
                    src = CT[:, ch, j:j + S]
                    w = col1(layer, "cw", 1, ch * TAPS + j)
                    if j == 0:
                        dve.tensor_scalar(Y[:, ch, :], src, w, col1(layer, "cb", 1, ch), ALU.mult,
                                          ALU.add).then_inc(conv_step, 1)
                    else:
                        dve.wait_ge(conv_step, layer * CC * TAPS + k - CC + 1)
                        dve.scalar_tensor_tensor(out=Y[:, ch, :], in0=src, scalar=w, in1=Y[:, ch, :],
                                                 op0=ALU.mult, op1=ALU.add).then_inc(conv_step, 1)

            def attention(units, between=None):
                u0 = c.unit
                xs = [c.pt]
                for un in units:
                    xs.append(xs[-1] + len(un["kbs"]))

                def mask(i):
                    u, un = u0 + i, units[i]
                    n, kl = len(un["scores"]), un["kl"]
                    dve.wait_ge(sc_full, u + 1)
                    if i >= 2:
                        dve.wait_ge(pt_full, xs[i - 1])
                    raw = PS[:, 2 * (u % 2):2 * (u % 2) + 2, :].rearrange("p b (m s) -> p (b m) s", s=S)[:, 0:n, 0:kl]
                    tile = SM[:, u % 2, 0:n, 0:kl]
                    if un["bias"] is None:
                        seq(dve.tensor_copy(tile, raw))
                    elif un["bias"][0] == "shared":
                        seq(dve.tensor_tensor(tile, raw, un["bias"][1].unsqueeze(1).to_broadcast([P, n, kl]), ALU.add))
                    else:
                        for m, s in enumerate(un["bias"][2]):
                            ins = dve.scalar_tensor_tensor(out=tile[:, m, :], in0=un["bias"][1], scalar=s,
                                                           in1=raw[:, m, :], op0=ALU.mult, op1=ALU.add)
                        seq(ins)
                    seq(dve.tensor_reduce(mx[:, u % 2, 0:n], tile, AX, ALU.max))
                    dve.tensor_scalar(nb[:, u % 2, 0:n], mx[:, u % 2, 0:n], -un["scale"], None,
                                      ALU.mult).then_inc(sm_ready, 1)

                def end(i):
                    u, un = u0 + i, units[i]
                    n, dv, t = len(un["scores"]), un["dv"], un["t"]
                    dve.wait_ge(o_full, u + 1)
                    cf = coef[:, u % 2, 0:n]
                    seq(dve.reciprocal(cf, sums[:, u % 4, 0:n]))
                    o = PS[:, 6 + u % 2, 0:n * dv].rearrange("p (m d) -> p m d", m=n)
                    kind = un["end"]
                    if kind[0] == "plain":
                        dst = H[:, t, kind[1]:kind[1] + n * dv].rearrange("p (m d) -> p m d", m=n)
                        dve.tensor_tensor(dst, o, bc4(cf, dv), ALU.mult).then_inc(o_out, 1)
                    elif kind[0] == "diff":
                        seq(dve.tensor_tensor(cf, cf, lam4[:], ALU.mult))
                        tmp = otmp[:].rearrange("p (m d) -> p m d", m=4)
                        seq(dve.tensor_tensor(tmp, o, bc4(cf, dv), ALU.mult))
                        pair = otmp[:].rearrange("p (h two d) -> p h two d", h=2, two=2)
                        dst = H[:, t, kind[1]:kind[1] + 128].rearrange("p (h d) -> p h d", h=2)
                        dve.tensor_tensor(dst, pair[:, :, 0, :], pair[:, :, 1, :], ALU.add).then_inc(o_out, 1)
                    else:
                        _, br, g = kind
                        gates = proj[:, t, GATE0:GATE0 + 24].rearrange("p (h b) -> p h b", b=3)[
                            :, g * QPK:(g + 1) * QPK, br]
                        seq(dve.tensor_tensor(cf, cf, gates, ALU.mult))
                        dst = H[:, t, g * QPK * HD:(g + 1) * QPK * HD].rearrange("p (m d) -> p m d", m=n)
                        if br == 0:
                            seq(dve.tensor_scalar(cf, cf, cvalid[:, t:t + 1], None, ALU.mult))
                            dve.tensor_tensor(dst, o, bc4(cf, dv), ALU.mult).then_inc(o_out, 1)
                        else:
                            tmp = otmp[:].rearrange("p (m d) -> p m d", m=4)
                            seq(dve.tensor_tensor(tmp, o, bc4(cf, dv), ALU.mult))
                            dve.tensor_tensor(dst, dst, tmp, ALU.add).then_inc(o_out, 1)

                for i in range(len(units) + 2):
                    if i < len(units):
                        mask(i)
                    if between is not None:
                        between(i, len(units) + 2)
                    if i >= 2:
                        end(i - 2)
                c.unit += len(units)
                c.pt = xs[-1]
                dve.wait_ge(o_out, c.unit)

            def ffn(chunks, gated):
                for j in range(chunks):
                    for t in range(T):
                        q = c.hid + 2 * j + t
                        dve.wait_ge(hid_act, q + 1)
                        if q >= 2:
                            dve.wait_ge(hid_tr, q - 1)
                        dve.tensor_tensor(hm[:, t, :], sil[:, t, :], PS[:, 2 * t + 1, :] if gated else sil[:, t, :],
                                          ALU.mult).then_inc(hid_rows, 1)
                c.hid += 2 * chunks
                c.down += chunks
                dve.wait_ge(down_done, c.down)
                for t in range(T):
                    for half in range(2):
                        row = X[:, t, half * 512:half * 512 + 512]
                        ins = dve.tensor_tensor(row, PS[:, 4 + 2 * t + half, :], row, ALU.add)
                seq(ins)

            def moe(layer):
                bank = bank_of()
                lg = rt8[:, 2:4, 0:8]
                dve.tensor_copy(lg, PS[:, bank, 0:16].rearrange("p (t e) -> p t e", t=T)).then_inc(lin_out, 1)
                dve.wait_ge(lin_out, c.lin)
                top = rt8[:, 4:6, 0:8]
                for t in range(T):
                    ins = dve.max(top[:, t, :], lg[:, t, :])
                seq(ins)
                for t in range(T):
                    ins = dve.max_index(idx8[:, t, :], top[:, t, :], lg[:, t, :])
                seq(ins)
                idf = rt8[:, 6, 0:4].rearrange("p (t k) -> p t k", t=T)
                seq(dve.tensor_copy(idf, idx8[:, :, 0:2]))
                for k in range(2):
                    for t in range(T):
                        ins = dve.tensor_scalar(rt8[:, 9 + 2 * k + t, 0:8], slot_no[:, 0:8], idf[:, t, k:k + 1], None,
                                                ALU.is_equal)
                seq(ins)
                dve.tensor_tensor(rt8[:, 0:2, 0:8], rt8[:, 9:11, 0:8], rt8[:, 11:13, 0:8], ALU.add).then_inc(router_a, 1)
                dve.tensor_tensor(rt8[:, 7, 0:T], top[:, :, 1], top[:, :, 0], ALU.subtract).then_inc(gate_in, 1)
                dve.wait_ge(gate_ok, 1)
                seq(dve.tensor_scalar(rt8[:, 13, 0:T], rt8[:, 8, 0:T], 1.0, None, ALU.add))
                seq(dve.reciprocal(rt8[:, 13, 0:T], rt8[:, 13, 0:T]))
                seq(dve.tensor_tensor(rt8[:, 14, 0:T], rt8[:, 8, 0:T], rt8[:, 13, 0:T], ALU.mult))
                for t in range(T):
                    ins = dve.tensor_scalar(g16[:, t, 0:8], rt8[:, 9 + t, 0:8], rt8[:, 13, t:t + 1], None, ALU.mult)
                seq(ins)
                for t in range(T):
                    ins = dve.scalar_tensor_tensor(out=g16[:, t, 0:8], in0=rt8[:, 11 + t, 0:8],
                                                   scalar=rt8[:, 14, t:t + 1], in1=g16[:, t, 0:8],
                                                   op0=ALU.mult, op1=ALU.add)
                seq(ins)
                seq(dve.tensor_copy(g16[:, :, 8:16], g16[:, :, 0:8]))
                bank = bank_of()
                seq(dve.scalar_tensor_tensor(out=rk[:, :, 0:8], in0=rt8[:, 0:2, 0:8], scalar=-1000.0,
                                             in1=PS[:, bank, 0:16].rearrange("p (t e) -> p t e", t=T),
                                             op0=ALU.mult, op1=ALU.add))
                dve.tensor_reduce(rt8[:, 15, 0:1], PS[:, bank, 16:24], AX, ALU.max).then_inc(lin_out, 1)
                dve.wait_ge(lin_out, c.lin)
                seq(dve.tensor_scalar(rk[:, :, 8:16], rk[:, :, 0:8], 1000.0 - SLOTS, None, ALU.add))
                seq(dve.tensor_scalar(rk[:, :, 0:8], rk[:, :, 0:8], 1000.0, None, ALU.add))
                seq(dve.tensor_scalar(rt8[:, 15, 1:2], rt8[:, 15, 0:1], float(SLOTS), 8.0, ALU.is_gt, ALU.mult))
                dve.tensor_scalar(nit[:, 1:2], rt8[:, 15, 1:2], 7.0, None, ALU.add)
                dve.tensor_scalar(nit[:, 0:1], rt8[:, 15, 1:2], 8.0, None, ALU.add).then_inc(routed, 1)
                dve.wait_ge(routed, 1)
                steps = dve.value_load(nit[0:1, 0:1], min_val=EXPERTS, max_val=2 * EXPERTS)
                gains = col1(layer, "ffn", 8)
                with dve.Fori(0, steps) as it:
                    for t in range(T):
                        ins = dve.tensor_scalar(disp[:, t, :], slot_no[:], rk[:, t, bass.ds(it, 1)], None, ALU.is_equal)
                    ins.then_inc(e_disp, 1)
                    for k in range(2):
                        dve.wait_ge(e_gath, it * 2 + (k + 1))
                        dve.tensor_tensor(xgT[:, 4 * k:4 * k + 4, :], PS[:, 6 + k, :].rearrange("p (k s) -> p k s", k=4),
                                          bc4(gains[:, 4 * k:4 * k + 4], P), ALU.mult).then_inc(e_xg, 1)
                    for j in range(J1):
                        dve.wait_ge(e_act, it * J1 + (j + 1))
                        if j >= 2:
                            dve.wait_ge(e_tr, it * J1 + (j - 1))
                        dve.tensor_tensor(hm[:, j % 2, :], sil[:, j % 2, :], PS[:, 2 * (j % 2) + 1, :],
                                          ALU.mult).then_inc(e_rows, 1)
                    for t in range(T):
                        for half in range(2):
                            k = 2 * t + half
                            dve.wait_ge(e_comb, it * 4 + (k + 1))
                            row = X[:, t, half * 512:half * 512 + 512]
                            dve.scalar_tensor_tensor(out=row, in0=PS[:, 6 + k % 2, :],
                                                     scalar=g16[:, t, bass.ds(it, 1)], in1=row, op0=ALU.mult,
                                                     op1=ALU.add).then_inc(e_acc, 1)
                    dve.wait_ge(e_acc, it * 4 + 4)

            dve.wait_ge(const_ok, CONST_OK)
            dve.wait_ge(const_ld, 16 * 6)
            dve.wait_ge(x_ld, 16)
            seq(dve.tensor_copy(posf[:, 0:5], posi[:, 0:5]))
            for t in range(T):
                dve.tensor_scalar(ang[:, t * 8:t * 8 + 8], inv[:, 0:8], posf[:, t:t + 1], None, ALU.mult)
                dve.tensor_scalar(ang[:, 24 + t * 16:40 + t * 16], inv[:, 8:24], posf[:, 2 + t:3 + t], None, ALU.mult)
            seq(dve.tensor_scalar(ang[:, 16:24], inv[:, 0:8], posf[:, 4:5], None, ALU.mult))
            turns = rt[:, 0:2, 0:56]
            phase = (0.0, float(np.float32(np.pi / 2)))
            magic = 12582912.0
            two_pi = 2.0 * np.pi
            p1 = float(np.float32(6.28125))
            p2 = float(np.float32(np.round((two_pi - p1) * 2 ** 20) / 2 ** 20))
            p3 = float(np.float32(two_pi - p1 - p2))
            for k in range(2):
                seq(dve.tensor_scalar(turns[:, k, :], ang[:], phase[k], 1.0 / two_pi, ALU.add, ALU.mult))
            seq(dve.tensor_scalar(turns, turns, magic, None, ALU.add))
            seq(dve.tensor_scalar(turns, turns, magic, None, ALU.subtract))
            seq(dve.tensor_copy(red[:], ang[:].unsqueeze(1).to_broadcast([P, 2, 56])))
            for part in (p1, p2, p3):
                seq(dve.scalar_tensor_tensor(out=red[:], in0=turns, scalar=-part, in1=red[:], op0=ALU.mult,
                                             op1=ALU.add))
            seq(dve.tensor_scalar(red[:, 1, :], red[:, 1, :], phase[1], None, ALU.add))
            lim = 3.1415925
            dve.tensor_scalar(red[:], red[:], lim, -lim, ALU.min, ALU.max).then_inc(trig_in, 1)
            seq(dve.tensor_copy(dist[:, 0, :], rowi[:]))
            seq(dve.tensor_scalar(dist[:, 1, :], dist[:, 0, :], posf[:, 3:4], None, ALU.subtract))
            seq(dve.tensor_scalar(dist[:, 0, :], dist[:, 0, :], posf[:, 2:3], None, ALU.subtract))
            seq(dve.scalar_tensor_tensor(out=dist[:], in0=dist[:], scalar=-1.0, in1=dist[:], op0=ALU.mult,
                                         op1=ALU.max))
            dve.tensor_tensor(dist[:, 1, :], dist[:, 1, :], causal[:], ALU.subtract)
            seq(dve.tensor_tensor(dist[:, 0, 0:P], dist[:, 0, 0:P], causal[:, P:S], ALU.subtract))
            dve.wait_ge(trig_ok, 1)

            def sin_cos(c0, n):
                return trig[:, 0, c0:c0 + n], trig[:, 1, c0:c0 + n]

            for layer in range(LAYERS):
                norm(X, col1(layer, "attn", 8))
                base = c.lin
                seq(dve.memset(CT[:, :, 0:TAPS - 1], 0.0))
                dve.wait_ge(lin_out, base + 4)
                dve.tensor_tensor(proj[:, :, GLU_A0:GLU_A0 + 512], proj[:, :, GLU_A0:GLU_A0 + 512],
                                  proj[:, :, GLU_G0:GLU_G0 + 512], ALU.mult).then_inc(rows_ready, 1)
                turn_base = c.turn
                dve.wait_ge(turn_out, turn_base + 2 + 2)
                for v in range(2):
                    for g in range(2):
                        for h in range(2):
                            src = QT[0:HD, 12 + 2 * v + g, 16 * h:16 * h + 240].rearrange("p (n b) -> p b n", b=16)
                            pe_ = cpos[:, layer, v, 16 * h:16 * h + 16]
                            ins = dve.tensor_tensor(kblk[:, v, 16 * h:16 * h + 16, g * NCMP:(g + 1) * NCMP], src,
                                                    bc4(pe_, NCMP), ALU.add)
                ins.then_inc(blk_ready, 1)
                dve.wait_ge(lin_out, base + 10)
                regions = [(Q0, 8, 0), (KSLC0, 2, 2), (KWIN0, 2, 3)]
                scr_sq = SM[:].rearrange("p a b c -> p (a b c)")
                o = 0
                for t in range(T):
                    for c0, n, gi in regions:
                        view = proj[:, t, c0:c0 + n * HD]
                        sq = scr_sq[:, 0:n * HD]
                        seq(dve.tensor_tensor(sq, view, view, ALU.mult))
                        seq(dve.tensor_reduce(st[:, o:o + n], sq.rearrange("p (h d) -> p h d", d=HD), AX, ALU.add))
                        o += n
                mean_eps(24, HD)
                o = 0
                for t in range(T):
                    sin, cos = sin_cos(t * 8, 8)
                    for c0, n, gi in regions:
                        view = proj[:, t, c0:c0 + n * HD].rearrange("p (h d) -> p h d", d=HD)
                        gain = bc[:, layer * B1W + gi * HD:layer * B1W + (gi + 1) * HD]
                        heads_norm(view, 0, n, HD, gain, o)
                        o += n
                        rotate(view[:, :, 0:8], view[:, :, 8:16], cos, sin, n, 8,
                               rows_ready if o == 24 else None)
                dve.wait_ge(lin_out, base + 13)
                kk = kc_sb[0:NCMP, 0:2, :]
                sq = scr_sq[0:NCMP, 0:2 * HD].rearrange("p (h d) -> p h d", d=HD)
                seq(dve.tensor_tensor(sq, kk, kk, ALU.mult))
                seq(dve.tensor_reduce(st[0:NCMP, 0:2], sq, AX, ALU.add))
                mean_eps(2, HD)
                heads_norm(kk, 0, 2, HD, bc[0:NCMP, layer * B1W + HD:layer * B1W + 2 * HD], 0)
                sin, cos = sin_cos(16, 8)
                rotate(kk[:, :, 0:8], kk[:, :, 8:16], cos[0:NCMP, :], sin[0:NCMP, :], 2, 8, rows_ready)

                def between(i, n):
                    k = CC * TAPS
                    conv_ops(layer, k * i // n, k * (i + 1) // n)

                c.turn += 2 + 2 + 6 + 1
                attention(nsa_units(), between)
                c.lin = base + 13
                bank = bank_of()
                mean = PS[:, bank, 0:S].unsqueeze(1).to_broadcast([P, CC, S])
                dve.tensor_tensor(Y, Y, mean, ALU.subtract).then_inc(lin_out, 1)
                dve.wait_ge(lin_out, c.lin)
                dve.tensor_tensor(SQ, Y, Y, ALU.mult).then_inc(ln_sq, 1)
                bank = bank_of()
                dve.tensor_scalar(lnv[:], PS[:, bank, 0:S], EPS, None, ALU.add).then_inc(lin_out, 1)
                dve.wait_ge(ln_ok, layer + 1)
                dve.tensor_tensor(Y, Y, rs[:].unsqueeze(1).to_broadcast([P, CC, S]), ALU.mult).then_inc(ln_fin, 1)
                c.turn += 2
                add_out()
                norm(X, col1(layer, "ffn", 8))
                if layer == 0:
                    ffn(J1, True)
                else:
                    moe(layer)

            for layer in range(LAYERS):
                norm(X, col2(layer, "attn", 8))
                base = c.lin
                b0 = 2 * B1W + layer * B2W
                for k in range(2):
                    lq, lk = (bc[:, b0 + HD + (2 * k + i) * DIFF_D:b0 + HD + (2 * k + i + 1) * DIFF_D] for i in range(2))
                    seq(dve.tensor_tensor_reduce(rt[:, k, 0:DIFF_D], lq, lk, 1.0, 0.0, ALU.mult, ALU.add,
                                                 lam[:, k:k + 1]))
                dve.tensor_copy(lam[:, 2:4], mhalf[:].to_broadcast([P, 2])).then_inc(lam_in, 1)
                dve.wait_ge(lam_ok, layer + 1)
                lam0 = 0.8 - 0.6 * float(np.exp(-0.3 * layer))
                seq(dve.tensor_tensor(lam[:, 2:3], lam[:, 1:2], lam[:, 0:1], ALU.subtract))
                seq(dve.memset(lam4[:], 1.0))
                for k in (1, 3):
                    ins = dve.tensor_scalar(lam4[:, k:k + 1], lam[:, 2:3], -lam0, None, ALU.add)
                seq(ins)
                dve.wait_ge(lin_out, base + 2)
                parts = [(t, c0, n, 2 * t + i) for t in range(T) for i, (c0, n) in enumerate(((0, QR), (CKV0, KVR)))]
                junk = SM[:].rearrange("p a b c -> p (a b c)")
                for t, c0, n, o in parts:
                    view = proj[:, t, c0:c0 + n]
                    seq(dve.tensor_tensor_reduce(junk[:, 0:n], view, view, 1.0 / n, 0.0, ALU.mult, ALU.add,
                                                 st[:, o:o + 1]))
                mean_eps(4, 1)
                for t, c0, n, o in parts:
                    view = proj[:, t, c0:c0 + n]
                    ins = dve.tensor_scalar(view, view, rs[:, o:o + 1], None, ALU.mult)
                ins.then_inc(rows_ready, 1)
                dve.wait_ge(lin_out, base + 18)
                for t in range(T):
                    sin, cos = sin_cos(24 + 16 * t, 16)
                    kr = proj[:, t, KR0:KR0 + MROPE].unsqueeze(1)
                    rotate(kr[:, :, 0:16], kr[:, :, 16:32], cos, sin, 1, 16)
                    q = QM[:, t, :, :]
                    rotate(q[:, :, NOPE:NOPE + 16], q[:, :, NOPE + 16:NOPE + 32], cos, sin, MLA_H, 16,
                           rows_ready if t == T - 1 else None)
                attention(mla_units())
                attention(diff_units())
                attention(moba_units())
                for t in range(T):
                    view = H[:, t, 384:768]
                    seq(dve.tensor_tensor(junk[:, 0:384], view, view, ALU.mult))
                    seq(dve.tensor_reduce(st[:, 6 * t:6 * t + 6], junk[:, 0:384].rearrange("p (h d) -> p h d", d=64),
                                          AX, ALU.add))
                mean_eps(12, 64)
                seq(dve.tensor_scalar(rs[:, 0:12], rs[:, 0:12], 1.0 - lam0, None, ALU.mult))
                for t in range(T):
                    view = H[:, t, 384:768].rearrange("p (h d) -> p h d", d=64)
                    seq(dve.tensor_tensor(view, view, bc4(rs[:, 6 * t:6 * t + 6], 64), ALU.mult))
                    ins = dve.tensor_tensor(view, view, bc[:, b0:b0 + 64].unsqueeze(1).to_broadcast([P, 6, 64]), ALU.mult)
                ins.then_inc(rows_ready, 1)
                c.lin = base + 18
                add_out()
                dve.wait_ge(mem_ld, 16 * (layer + 1))
                norm(MEM, col2(layer, "mem", 8))
                norm(X, col2(layer, "cross", 8))
                attention(cross_units())
                c.lin += 12
                add_out()
                norm(X, col2(layer, "mlp", 8))
                ffn(J2, False)
            norm(X)
            dve.wait_ge(norm_rows, 2 * c.norm + 2)
            dve.wait_ge(fin_ld, 16)
            dve.tensor_tensor(H[:], H[:], MEM[:, 0, :].unsqueeze(1).to_broadcast([P, T, D]), ALU.mult).then_inc(x_done, 1)


WEIGHTS = ["w_in", "w_out", "cmp_w1_k", "cmp_w1_v", "ffn_w_gate", "ffn_w_up", "ffn_w_down", "moe_w_gate", "moe_w_up",
           "moe_w_down", "w_in_2", "mla_w_uq_2", "mla_w_ukv_2", "w_out_2", "cross_wq_2", "cross_wkv_2", "cross_wo_2",
           "mlp_w1_2", "mlp_w2_2", "x", "mem_2", "positions_2", "final_norm_2"]


def by_partition(v):
    return v.reshape(-1, P).T


def kernel(**inputs):
    import concourse.bacc as bacc
    from concourse.bass_utils import run_bass_kernel_spmd

    x = {k: np.asarray(v) for k, v in inputs.items()}
    arrays = {k: np.ascontiguousarray(x[k]) for k in WEIGHTS}
    arrays["final_norm_2"] = arrays["final_norm_2"].reshape(1, D)
    cols = []
    for l in range(LAYERS):
        cols += [by_partition(x[k][l]) for k in ("attn_norm_g", "ffn_norm_g", "conv_b", "conv_ln_g", "conv_ln_b")]
        cols.append(x["conv_w"][l].reshape(TAPS, CC, P).transpose(2, 1, 0).reshape(P, CC * TAPS))
    for l in range(LAYERS):
        cols += [by_partition(x[k][l]) for k in ("attn_norm_2", "cross_norm_2", "mem_norm_2", "mlp_norm_2",
                                                 "mla_q_norm_2", "mla_kv_norm_2")]
    cols.append(x["moe_router"][0].reshape(KC, P, EXPERTS).transpose(1, 0, 2).reshape(P, KC * EXPERTS))
    arrays["cols"] = np.ascontiguousarray(np.concatenate(cols, axis=1))
    rows = []
    for l in range(LAYERS):
        rows += [x["q_norm_g"][l], x["k_norm_g"][l].reshape(-1)]
    for l in range(LAYERS):
        rows += [x["diff_sub_norm_2"][l]] + [x[f"diff_lambda_{k}_2"][l] for k in ("q1", "k1", "q2", "k2")]
    arrays["bc"] = np.ascontiguousarray(np.concatenate(rows)[None, :])
    arrays["cpos"] = np.ascontiguousarray(
        np.stack([x["cmp_pos_k"], x["cmp_pos_v"]], axis=1).transpose(3, 0, 1, 2))
    arrays["cw2"] = np.ascontiguousarray(np.stack([x["cmp_w2_k"], x["cmp_w2_v"]], axis=1).transpose(2, 0, 1, 3))
    posc = np.zeros((P, 5), np.int32)
    posc[:, 0:2] = by_partition(x["positions"][0])
    posc[:, 2:4] = by_partition(x["positions_2"][0])
    posc[0:NCMP, 4] = x["positions"][0, CMP_LEN - 1::CMP_STRIDE]
    arrays["posc"] = posc

    nc = bacc.Bacc("TRN2", target_bir_lowering=False, num_devices=1, dynamic_dma_scratch_size=1024)
    aps = {k: nc.dram_tensor(f"in_{k}", v.shape, mybir.dt.from_np(v.dtype), kind="ExternalInput").ap()
           for k, v in arrays.items()}
    out = nc.dram_tensor("out_0", (1, S, D), F32, kind="ExternalOutput").ap()
    build(nc, aps, out)
    r = run_bass_kernel_spmd(nc, [{f"in_{k}": v for k, v in arrays.items()}], core_ids=[0])
    return r.results[0]["out_0"]
```

```python
from contextlib import ExitStack

import numpy as np

import concourse.bass as bass
from concourse import mybir

F32 = mybir.dt.float32
F32R = mybir.dt.float32r
I32 = mybir.dt.int32
U32 = mybir.dt.uint32
ALU = mybir.AluOpType
ACT = mybir.ActivationFunctionType
AX = mybir.AxisListType.X

P = 128
S = 256
T = S // P
D = 1024
KC = D // P
LAYERS = 2
EPS = 1e-6
MASKED = -1e30
BANK = 512

HEADS, KV_HEADS, HD = 8, 2, 64
QPK = HEADS // KV_HEADS
CMP_LEN, CMP_STRIDE, CMP_HID = 32, 16, 128
NCMP = (S - CMP_LEN) // CMP_STRIDE + 1
CONV_CH, TAPS = 512, 31
CC = CONV_CH // P
PE_TAPS = 28
CONV_OPS = [(j, ch) for j in range(TAPS) for ch in range(CC - 1)] + [(j, CC - 1) for j in range(PE_TAPS, TAPS)]
Q0, KCMP0, VCMP0, KSLC0, VSLC0, KWIN0, VWIN0, GATE0, GLU_A0, GLU_G0 = (
    0, 512, 640, 768, 896, 1024, 1152, 1280, 1304, 1816)
IN1 = 2328
F1 = 3584
J1 = F1 // 512
EXPERTS = 8
SLOTS = P

MLA_H, NOPE, MROPE, MLA_V, QR, KVR = 6, 64, 32, 64, 256, 128
DIFF_H, DIFF_D = 6, 32
MOBA_H = 4
CROSS_H, CROSS_D = 4, 256
CKV0, KR0, DQ0, DK0, DV0, MQ0, MK0, MV0 = 256, 384, 416, 800, 1184, 1568, 1824, 2080
IN2 = 2336
J2 = 4096 // 512
SLOPES = [2.0 ** (-8.0 * (h + 1) / (DIFF_H + MOBA_H)) for h in range(DIFF_H + MOBA_H)]

RING = 7
SPLITS = 3
AHEAD = SPLITS - 1
PIECE = 2048
HALF = KC // 2
MOE_PIECES = 6 * J1
MOE_HALVES = 4 * J1

C1 = dict(attn=0, ffn=8, cb=16, lng=20, lnb=24, cw=28)
C1W = 28 + CC * TAPS
C2 = dict(attn=0, cross=8, mem=16, mlp=24, qn=32, kvn=34)
C2W = 35
B1W = 4 * HD
B2W = HD + 4 * DIFF_D


class Count:

    def __init__(self):
        self.raw = self.split = self.piece = self.half = self.lin = self.turn = self.mix = 0
        self.norm = self.seen = self.pow = self.unit = self.pt = self.hid = self.down = self.ffn = self.misc = 0


def build(nc, a, out):
    ctx = ExitStack()
    with ctx:
        def sb(name, shape, dt=F32):
            return ctx.enter_context(nc.sbuf_tensor(name, shape, dt))

        def sem(name):
            return ctx.enter_context(nc.semaphore(name))

        PS = ctx.enter_context(nc.psum_tensor("PS", [P, 8, BANK], F32))

        ring = sb("ring", [P, RING, PIECE])
        Wh = sb("Wh", [P, SPLITS, PIECE], F32R)
        Wl = sb("Wl", [P, SPLITS, PIECE], F32R)
        X = sb("X", [P, T, D])
        H = sb("H", [P, T, D])
        HTh = sb("HTh", [P, KC, S], F32R)
        latent_at = nc.sbuf_base
        HTl = sb("HTl", [P, KC, S], F32R)
        lat = nc.alloc_sbuf_tensor_at("lat", [P, KC * S], F32, offset=latent_at)
        proj = sb("proj", [P, T, IN2])
        scr_at = nc.sbuf_base
        scr = sb("scr", [P, 6656])

        def over_scr(name, first, shape):
            return nc.alloc_sbuf_tensor_at(name, shape, F32R, offset=scr_at + 4 * first)

        SM = sb("SM", [P, 2, 4, S])
        PT = sb("PT", [P, 2, 2, 4, P])
        ident = sb("ident", [P, P])
        ones = sb("ones", [P, P])
        mean_w = sb("mean_w", [P, P])
        before = sb("before", [P, P])
        slot_no = sb("slot_no", [P, P])
        causal = sb("causal", [P, S])
        cmask = sb("cmask", [P, T, 16])
        cvalid = sb("cvalid", [P, T])
        dist = sb("dist", [P, T, S])
        mhalf = sb("mhalf", [P, 1])
        cols = sb("cols", [P, 2 * C1W + 2 * C2W + EXPERTS * KC])
        bc = sb("bc", [P, 2 * B1W + 2 * B2W])
        cpos = sb("cpos", [HD, LAYERS, 2, CMP_LEN])
        cw2 = sb("cw2", [P, LAYERS, 2, HD])
        rw_hi = sb("rw_hi", [P, KC, EXPERTS], F32R)
        rw_lo = sb("rw_lo", [P, KC, EXPERTS], F32R)
        posi = sb("posi", [P, 8], I32)
        posf = sb("posf", [P, 8])
        rowi = sb("rowi", [P, S], I32)
        inv = sb("inv", [P, 24])
        ang = sb("ang", [P, 56])
        red = sb("red", [P, 2, 56])
        trig = sb("trig", [P, 2, 56])
        st = sb("st", [P, 48])
        sumsq = sb("sumsq", [P, 2, T])
        diag = sb("diag", [P, T, P])
        rs = sb("rs", [P, 48])
        rt = sb("rt", [P, 4, 192])
        mx = sb("mx", [P, 2, 4])
        nb = sb("nb", [P, 2, 4])
        sums = sb("sums", [P, 4, 4])
        coef = sb("coef", [P, 2, 4])
        otmp = sb("otmp", [P, 4 * HD])
        hid = sb("hid", [P, 2, 30])
        kc_sb = sb("kc_sb", [16, 4, HD])
        kcT = sb("kcT", [HD, 2, 16])
        lam = sb("lam", [P, 4])
        lam4 = sb("lam4", [P, 4])
        nit = sb("nit", [P, 2], I32)
        rt8 = sb("rt8", [P, 16, 16])
        idx8 = sb("idx8", [P, T, 8], U32)
        rk = sb("rk", [P, T, 17])
        gate = sb("gate", [P, T, 17])

        taps_h = H[:].rearrange("p t d -> p (t d)").rearrange("p (j s) -> p j s", s=P)
        taps_s = SM[:].rearrange("p a b s -> p (a b s)").rearrange("p (j s) -> p j s", s=P)

        def tap_matrix(j):
            return taps_h[:, j, :] if j < T * KC else taps_s[:, j - T * KC + 4, :]

        hid_rows_sb = otmp[0:2 * NCMP, :].rearrange("p (v h) -> p v h", v=2)
        QT = scr[:, 0:24 * S].rearrange("p (m s) -> p m s", s=S)
        CT = scr[:, 4096:4096 + CC * (S + TAPS - 1)].rearrange("p (c s) -> p c s", c=CC)
        Y = scr[:, 5248:5248 + CC * S].rearrange("p (c s) -> p c s", c=CC)
        SQ = scr[:, 4096:4096 + CC * S].rearrange("p (c s) -> p c s", c=CC)
        kblk = PT[:].rearrange("p a b c d -> p (a b c d)")[0:HD, 0:2 * CMP_LEN * 30].rearrange(
            "p (v l n) -> p v l n", v=2, l=CMP_LEN)
        QM = lat[:, 0:T * MLA_H * 96].rearrange("p (t h d) -> p t h d", t=T, h=MLA_H)
        CQT = lat[:, 1152:1152 + 3 * S].rearrange("p (k s) -> p k s", s=S)
        KVH = scr[:, 19 * S:19 * S + T * MLA_H * P].rearrange("p (t n) -> p t n", t=T)
        MEM = scr[:, 0:T * D].rearrange("p (t d) -> p t d", t=T)
        CQ = MEM
        CQT8 = scr[:, 2048:4096].rearrange("p (k s) -> p k s", s=S)
        CKT8 = scr[:, 4096:6144].rearrange("p (k s) -> p k s", s=S)
        projf = proj[:].rearrange("p t n -> p (t n)")
        sil = projf[:, 0:1024].rearrange("p (t n) -> p t n", t=T)
        hm = projf[:, 1024:2048].rearrange("p (t n) -> p t n", t=T)
        hTh = over_scr("hTh", 1024, [P, 4, S])
        hTl = over_scr("hTl", 2048, [P, 4, S])
        ye = scr[:, 0:1024]
        xgh = over_scr("xgh", 1024, [P, KC, P])
        xgl = over_scr("xgl", 2048, [P, KC, P])
        hmh = over_scr("hmh", 3072, [P, 4, P])
        hml = over_scr("hml", 3584, [P, 4, P])
        disp = scr[:, 4096:4352].rearrange("p (t s) -> p t s", t=T)
        dispT = scr[:, 4352:4608].rearrange("p (t s) -> p t s", t=T)

        const_ld = sem("const_ld")
        x_ld = sem("x_ld")
        const_ok = sem("const_ok")
        w_ld = [sem(f"w_ld{s}") for s in range(RING)]
        w_hi = sem("w_hi")
        w_lo = sem("w_lo")
        w_half = sem("w_half")
        lin_full = sem("lin_full")
        lin_out = sem("lin_out")
        turned = sem("turned")
        turn_out = sem("turn_out")
        pow_in = sem("pow_in")
        pow_out = sem("pow_out")
        norm_rows = sem("norm_rows")
        norm_tr = sem("norm_tr")
        norm_hi = sem("norm_hi")
        norm_T = sem("norm_T")
        mix_hi = sem("mix_hi")
        sc_full = sem("sc_full")
        sm_ready = sem("sm_ready")
        p_ready = sem("p_ready")
        pt_full = sem("pt_full")
        pt_out = sem("pt_out")
        o_full = sem("o_full")
        o_out = sem("o_out")
        hid_full = sem("hid_full")
        hid_act = sem("hid_act")
        hid_rows = sem("hid_rows")
        hid_tr = sem("hid_tr")
        hid_hi = sem("hid_hi")
        hid_T = sem("hid_T")
        down_done = sem("down_done")
        down_first = sem("down_first")
        rows_ready = sem("rows_ready")
        conv_step = sem("conv_step")
        taps_ready = sem("taps_ready")
        blk_ready = sem("blk_ready")
        ln_sq = sem("ln_sq")
        ln_diag = sem("ln_diag")
        mixT_hi = sem("mixT_hi")
        mixT_ok = sem("mixT_ok")
        lam_in = sem("lam_in")
        lam_ok = sem("lam_ok")
        trig_in = sem("trig_in")
        trig_ok = sem("trig_ok")
        mem_ld = sem("mem_ld")
        fin_ld = sem("fin_ld")
        x_done = sem("x_done")
        gate_in = sem("gate_in")
        gate_ok = sem("gate_ok")
        routed = sem("routed")
        router_a = sem("router_a")
        e_ld = [sem(f"e_ld{s}") for s in range(RING)]
        e_hi = sem("e_hi")
        e_lo = sem("e_lo")
        e_half = sem("e_half")
        e_disp = sem("e_disp")
        e_gath = sem("e_gath")
        e_xh = sem("e_xh")
        e_xg = sem("e_xg")
        e_dt = sem("e_dt")
        e_dts = sem("e_dts")
        e_gu = sem("e_gu")
        e_act = sem("e_act")
        e_rows = sem("e_rows")
        e_tr = sem("e_tr")
        e_th = sem("e_th")
        e_T = sem("e_T")
        e_down = sem("e_down")
        e_y = sem("e_y")
        e_comb = sem("e_comb")
        e_acc = sem("e_acc")
        dve_seq = sem("dve_seq")
        pool_seq = sem("pool_seq")
        out_st = sem("out_st")

        def col1(layer, name, n=1, off=0):
            c = layer * C1W + C1[name] + off
            return cols[:, c:c + n]

        def col2(layer, name, n=1, off=0):
            c = 2 * C1W + layer * C2W + C2[name] + off
            return cols[:, c:c + n]

        router_w = cols[:, 2 * (C1W + C2W):].rearrange("p (k e) -> p k e", e=EXPERTS)

        def raw_slot(r, k, n, rows=P):
            return ring[0:rows, r % RING, 0:k * n].rearrange("p (k n) -> p k n", k=k)

        def split_slot(i, k, n):
            return [w[:, i % SPLITS, 0:k * n].rearrange("p (k n) -> p k n", k=k) for w in (Wh, Wl)]

        def bc4(ap, n):
            return ap.unsqueeze(2).to_broadcast([ap.shape[0], ap.shape[1], n])

        def unit(t, kl, scores, bias, scale, values, dv, end, kbs=None):
            return dict(t=t, kl=kl, scores=scores, bias=bias, scale=scale, values=values, dv=dv,
                        end=end, kbs=kbs or [P] * (kl // P))

        def tok(t):
            return slice(t * P, t * P + P)

        def nsa_units():
            out_ = []
            for br in range(3):
                for g in range(KV_HEADS):
                    for t in range(T):
                        heads = range(g * QPK, g * QPK + QPK)
                        if br == 0:
                            kl = NCMP
                            sc = [[(QT[0:HD, h, tok(t)], kcT[:, g, 0:NCMP])] for h in heads]
                            val = [[kc_sb[0:NCMP, 2 + g, :]] for _ in heads]
                            bias = ("shared", cmask[:, t, 0:NCMP])
                            kbs = [NCMP]
                        else:
                            kl = (t + 1) * P
                            kslot = (8 if br == 1 else 10) + g
                            v0 = (VSLC0 if br == 1 else VWIN0) + g * HD
                            sc = [[(QT[0:HD, h, tok(t)], QT[0:HD, kslot, 0:kl])] for h in heads]
                            val = [[proj[:, kb, v0:v0 + HD] for kb in range(t + 1)] for _ in heads]
                            bias = ("shared", causal[:, S - kl:])
                            kbs = None
                        out_.append(unit(t, kl, sc, bias, HD ** -0.5, val, HD, ("nsa", br, g), kbs))
            return out_

        def mla_units():
            out_ = []
            for h0, n in ((0, 4), (4, 2)):
                for t in range(T):
                    kl = (t + 1) * P
                    hs = range(h0, h0 + n)
                    sc = [[(QT[0:NOPE, h, tok(t)], QT[0:NOPE, 12 + h, 0:kl]),
                           (QT[0:MROPE, 6 + h, tok(t)], QT[0:MROPE, 18, 0:kl])] for h in hs]
                    val = [[KVH[:, kb, h * P + NOPE:h * P + P] for kb in range(t + 1)] for h in hs]
                    out_.append(unit(t, kl, sc, ("shared", causal[:, S - kl:]), 96 ** -0.5, val, MLA_V,
                                     ("plain", h0 * MLA_V)))
            return out_

        def diff_units():
            out_ = []
            for g in range(3):
                for t in range(T):
                    kl = (t + 1) * P
                    ms = range(4 * g, 4 * g + 4)
                    sc = [[(QT[0:DIFF_D, m, tok(t)], QT[0:DIFF_D, 12 + m, 0:kl])] for m in ms]
                    val = [[proj[:, kb, DV0 + (m // 2) * 64:DV0 + (m // 2) * 64 + 64]
                            for kb in range(t + 1)] for m in ms]
                    scale = DIFF_D ** -0.5
                    bias = ("slopes", dist[:, t, 0:kl], [-SLOPES[m // 2] / scale for m in ms])
                    out_.append(unit(t, kl, sc, bias, scale, val, 64, ("diff", 384 + g * 128)))
            return out_

        def moba_units():
            out_ = []
            for t in range(T):
                kl = (t + 1) * P
                sc = [[(QT[0:64, m, tok(t)], QT[0:64, 4 + m, 0:kl])] for m in range(MOBA_H)]
                val = [[proj[:, kb, MV0 + m * 64:MV0 + m * 64 + 64] for kb in range(t + 1)]
                       for m in range(MOBA_H)]
                scale = 64 ** -0.5
                bias = ("slopes", dist[:, t, 0:kl], [-SLOPES[DIFF_H + m] / scale for m in range(MOBA_H)])
                out_.append(unit(t, kl, sc, bias, scale, val, 64, ("plain", 768)))
            return out_

        def cross_units():
            out_ = []
            for g in range(2):
                for t in range(T):
                    hs = (2 * g, 2 * g + 1)
                    sc = [[(CQT8[:, 2 * h + c, tok(t)], CKT8[:, 2 * h + c, :]) for c in range(2)] for h in hs]
                    val = [[proj[:, kb, D + h * CROSS_D:D + (h + 1) * CROSS_D] for kb in range(2)] for h in hs]
                    out_.append(unit(t, S, sc, None, CROSS_D ** -0.5, val, CROSS_D,
                                     ("plain", 2 * g * CROSS_D)))
            return out_

        def heads_batch(src, base, width, n_heads, dst0, dst=None):
            out_ = []
            for h in range(0, n_heads, 2):
                k = min(2, n_heads - h)
                srcs = [src[:, t, base + (h + i) * width:base + (h + i + 1) * width]
                        for i in range(k) for t in range(T)]
                target = QT if dst is None else dst
                out_.append((srcs, target[0:width, dst0 + h:dst0 + h + k, :], None))
            return out_

        QMf = QM.rearrange("p t h d -> p t (h d)")
        t_conv = []
        for c in range(0, CC, 2):
            t_conv.append(([proj[:, t, GLU_A0 + (c + i) * P:GLU_A0 + (c + i + 1) * P]
                            for i in range(2) for t in range(T)],
                           CT[:, c:c + 2, TAPS - 1:TAPS - 1 + S], None))
        t_cmp = heads_batch(proj, KCMP0, HD, 4, 12)
        t_nsa = (heads_batch(proj, Q0, HD, 8, 0) + heads_batch(proj, KSLC0, HD, 2, 8)
                 + heads_batch(proj, KWIN0, HD, 2, 10))
        t_hid = [([hid_rows_sb[:, v, :] for v in range(2)], hid[:], None)]
        t_kc = [([kc_sb[0:NCMP, g, :] for g in range(2)], kcT[:, :, 0:NCMP], None)]
        t_mix1, t_mix1_lo = (heads_batch(H, 0, P, 4, 0, dst) for dst in (HTh, HTl))
        t_mix2, t_mix2_lo = (heads_batch(H, 0, P, 8, 0, dst) for dst in (HTh, HTl))
        t_cross = heads_batch(CQ, 0, P, 8, 0, CQT8) + heads_batch(proj, 0, P, 8, 0, CKT8)
        t_mla = []
        for src, base, width, step, n, dst0 in ((QMf, 0, NOPE, 96, 6, 0), (QMf, NOPE, MROPE, 96, 6, 6),
                                                (KVH, 0, NOPE, P, 6, 12), (proj, KR0, MROPE, 0, 1, 18)):
            for h in range(0, n, 2):
                k = min(2, n - h)
                t_mla.append(([src[:, t, base + (h + i) * step:base + (h + i) * step + width]
                               for i in range(k) for t in range(T)], QT[0:width, dst0 + h:dst0 + h + k, :], None))
        t_diff = heads_batch(proj, DQ0, DIFF_D, 12, 0) + heads_batch(proj, DK0, DIFF_D, 12, 12)
        t_moba = heads_batch(proj, MQ0, 64, 4, 0) + heads_batch(proj, MK0, 64, 4, 4)

        def t_latent(layer):
            return [([proj[:, t, k * P:k * P + P] for t in range(T)], CQT[:, k:k + 1, :],
                     col2(layer, "qn", 1, k) if k < 2 else col2(layer, "kvn")) for k in range(3)]

        IN1_BLOCKS = [(GLU_A0, 512), (GLU_G0, 512), (0, 512), (512, 512), (1024, 280)]
        IN2_BLOCKS = [(0, 416), (416, 512), (928, 512), (1440, 512), (1952, 384)]

        raw_of, size_of, pe_done = [], [], []

        def plan():
            c = Count()

            def split(size, done=None):
                if done is None:
                    c.half += 1
                    done = (w_half, c.half)
                raw_of.append(c.raw)
                size_of.append(size)
                pe_done.append(done)
                c.raw += 1

            def linear(widths):
                for n in widths:
                    split(HALF * n)
                    c.lin += T
                    split(HALF * n, (lin_full, c.lin))

            def ffn(chunks, parts):
                for j in range(chunks + 1):
                    if j < chunks:
                        for i in range(2 * parts):
                            last = i == 2 * parts - 1
                            split(PIECE, (hid_full, c.hid + 2 * (j + 1)) if last else None)
                    if j >= 1:
                        split(PIECE)
                        split(PIECE, (down_done, c.down + j))
                c.hid += 2 * chunks
                c.down += chunks

            for layer in range(LAYERS):
                linear([n for _, n in IN1_BLOCKS])
                c.raw += 4
                c.lin += 1 + 3 + 3
                linear([512, 512])
                if layer == 0:
                    ffn(J1, 2)
            before_moe = len(raw_of)
            c.lin += 2
            for layer in range(LAYERS):
                linear([n for _, n in IN2_BLOCKS])
                c.raw += 2
                c.lin += 4 * T
                linear([512] * 10)
                ffn(J2, 1)
            return before_moe

        before_moe = plan()
        expert = []
        for j in range(J1):
            expert += [(g, j, half) for g in range(2) for half in range(2)]
            if j >= 1:
                expert += [(2, j - 1, half) for half in range(2)]
        expert += [(2, J1 - 1, half) for half in range(2)]
        halves = np.cumsum([not (kind >= 1 and half == 1) for kind, j, half in expert]).tolist()
        assert len(expert) == MOE_PIECES and halves[-1] == MOE_HALVES
        assert MOE_PIECES % RING == 0 and MOE_PIECES % SPLITS == 0

        def at_gate_up(j):
            return 6 * j + 2 if j else 4

        def after_hidden(j, parts):
            return 2 * parts * (j + 1) + 2 * max(j - 1, 0)

        block = ctx.enter_context(nc.Block())

        @block.sync
        def _(sp):
            c = Count()
            freed = range(0)
            users = []

            def load(src, k, n, rows=P):
                r = len(users)
                if r >= RING and r - RING not in freed:
                    sp.wait_ge(*users[r - RING])
                sp.dma_start(raw_slot(r, k, n, rows), src).then_inc(w_ld[r % RING], 16)

            def rows_of(w, k0, k, c0, n):
                return w[k0:k0 + k * P, c0:c0 + n].rearrange("(k p) n -> p k n", p=P)

            def split(src, k, n):
                load(src, k, n)
                c.split += 1
                users.append((w_lo, c.split))

            def lin_block(w, c0, n):
                for half in range(2):
                    split(rows_of(w, half * HALF * P, HALF, c0, n), HALF, n)
                c.lin += T

            def plain(src, k, n, outs, rows=P):
                load(src, k, n, rows)
                users.append((lin_full, c.lin + outs))

            def ffn(ws, wd, chunks):
                for j in range(chunks + 1):
                    if j < chunks:
                        for w in ws:
                            for half in range(2):
                                split(rows_of(w, half * HALF * P, HALF, j * 512, 512), HALF, 512)
                    if j >= 1:
                        for half in range(2):
                            split(rows_of(wd, (j - 1) * 512 + half * 256, 2, 0, D), 2, D)

            sp.dma_start(X[:], a["x"].rearrange("b (t p) d -> p (b t) d", p=P)).then_inc(x_ld, 16)
            sp.dma_start(cols[:], a["cols"]).then_inc(const_ld, 16)
            sp.dma_start(bc[:], a["bc"].to_broadcast([P, a["bc"].shape[1]])).then_inc(const_ld, 16)
            sp.dma_start(cpos[:], a["cpos"]).then_inc(const_ld, 16)
            sp.dma_start(cw2[:], a["cw2"]).then_inc(const_ld, 16)
            sp.dma_start(posi[:, 0:5], a["posc"]).then_inc(const_ld, 16)
            sp.dma_start(rowi[:], a["positions_2"].to_broadcast([P, S])).then_inc(const_ld, 16)

            for layer in range(LAYERS):
                w = a["w_in"][layer]
                for c0, n in IN1_BLOCKS:
                    lin_block(w, c0, n)
                for i, name in enumerate(("cmp_w1_k", "cmp_w1_v")):
                    w1 = a[name][layer].rearrange("(l d) h -> d l h", d=HD)
                    for half in range(2):
                        plain(w1[:, half * CMP_STRIDE:(half + 1) * CMP_STRIDE, :], CMP_STRIDE, CMP_HID, i + 2, HD)
                c.lin += 1 + 3 + 3
                for n in range(2):
                    lin_block(a["w_out"][layer], n * 512, 512)
                if layer == 0:
                    ffn([a["ffn_w_gate"][0], a["ffn_w_up"][0]], a["ffn_w_down"][0], J1)
            base = len(users)
            c.lin += 2

            def moe_src(e, i):
                kind, j, half = expert[i]
                if kind < 2:
                    w3 = a["moe_w_gate"] if kind == 0 else a["moe_w_up"]
                    return w3[0].rearrange("e d f -> (e d) f")[
                        bass.ds(e * D, D), j * 512:j * 512 + 512].rearrange(
                            "(k p) f -> p k f", p=P)[:, half * HALF:(half + 1) * HALF, :]
                return a["moe_w_down"][0].rearrange("e f d -> (e f) d")[
                    bass.ds(e * F1 + j * 512, 512), :].rearrange(
                        "(k p) f -> p k f", p=P)[:, 2 * half:2 * half + 2, :]

            def moe_dst(i):
                k, n = (HALF, 512) if expert[i % MOE_PIECES][0] < 2 else (2, D)
                return raw_slot(base + i, k, n)

            for i in range(RING):
                sp.wait_ge(*users[base + i - RING])
                sp.dma_start(moe_dst(i), moe_src(0, i)).then_inc(e_ld[(base + i) % RING], 16)
            sp.wait_ge(routed, 1)
            last = sp.value_load(nit[0:1, 1:2], min_val=EXPERTS - 1, max_val=2 * EXPERTS - 1)
            first_down = [p[0] for p in expert].index(2)
            with sp.Fori(0, last) as it:
                e0 = sp.snap(it & 7)
                e1 = sp.snap((it + 1) & 7)
                for e, i in ((e0, 0), (e0, first_down), (e1, 0), (e1, first_down)):
                    sp.lower_ap_dma(moe_src(e, i))
                for i in range(RING, MOE_PIECES + RING):
                    done = sp.snap(it * MOE_PIECES + (i - RING + 1))
                    sp.to_reg(done)
                    e = e0 if i < MOE_PIECES else e1
                    sp.wait_ge(e_lo, done)
                    sp.dma_start(moe_dst(i), moe_src(e, i % MOE_PIECES)).then_inc(e_ld[(base + i) % RING], 16)
            for i in range(RING, MOE_PIECES):
                done = sp.snap(last * MOE_PIECES + (i - RING + 1))
                sp.to_reg(done)
                sp.wait_ge(e_lo, done)
                sp.dma_start(moe_dst(i), moe_src(EXPERTS - 1, i)).then_inc(e_ld[(base + i) % RING], 16)
            done = sp.snap(last * MOE_PIECES + MOE_PIECES)
            sp.to_reg(done)
            sp.wait_ge(e_lo, done)
            freed = range(base - RING, base)

            for layer in range(LAYERS):
                w = a["w_in_2"][layer]
                for c0, n in IN2_BLOCKS:
                    lin_block(w, c0, n)
                plain(rows_of(a["mla_w_uq_2"][layer], 0, 2, 0, 576), 2, 576, 2 * T)
                plain(rows_of(a["mla_w_ukv_2"][layer], 0, 1, 0, 768), 1, 768, 4 * T)
                c.lin += 4 * T
                for n in range(2):
                    lin_block(a["w_out_2"][layer], n * 512, 512)
                sp.wait_ge(o_full, 24 + c.unit + 12)
                sp.dma_start(MEM, a["mem_2"].rearrange("b (t p) d -> p (b t) d", p=P)).then_inc(mem_ld, 16)
                c.unit += 16
                for name, blocks in (("cross_wkv_2", 4), ("cross_wq_2", 2), ("cross_wo_2", 2)):
                    for n in range(blocks):
                        lin_block(a[name][layer], n * 512, 512)
                ffn([a["mlp_w1_2"][layer]], a["mlp_w2_2"][layer], J2)
            sp.wait_ge(o_full, 24 + c.unit)
            sp.dma_start(MEM[:, 0, :], a["final_norm_2"].to_broadcast([P, D])).then_inc(fin_ld, 16)
            for t in range(T):
                sp.wait_ge(x_done, t + 1)
                sp.dma_start(out[0, tok(t), :], H[:, t, :]).then_inc(out_st, 16)
            sp.wait_ge(out_st, 16 * T)

        @block.gpsimd
        def _(pool):
            c = Count()

            def power(*widths):
                for n in widths:
                    c.pow += 1
                    pool.wait_ge(pow_in, c.pow)
                    pool.tensor_tensor(rs[:, 0:n], st[:, 0:n], mhalf[:].to_broadcast([P, n]),
                                       ALU.pow).then_inc(pow_out, 1)

            n = 0
            for tile, v in ((ident, 0.0), (ones, 1.0), (mean_w, 1.0 / CONV_CH), (before, 1.0),
                            (causal, 0.0), (cmask, 0.0), (cvalid, 1.0), (mhalf, -0.5), (st, 1.0), (ang, 0.0),
                            (posf, 0.0), (kc_sb, 0.0)):
                pool.memset(tile[:], v).then_inc(pool_seq, 1)
                n += 1
            half1 = np.float32(500000.0) ** (-2.0 * np.arange(8, dtype=np.float32) / np.float32(16))
            half2 = np.float32(10000.0) ** (-np.arange(16, dtype=np.float32) / np.float32(16))
            for i, v in enumerate(list(half1) + list(half2)):
                pool.memset(inv[:, i:i + 1], float(np.float32(v))).then_inc(pool_seq, 1)
                n += 1
            pool.wait_ge(pool_seq, n)
            pool.affine_select(out=ident[:], in_=ident[:], compare_op=ALU.not_equal, fill=1.0, base=0,
                               pattern=[[-1, P]], channel_multiplier=1).then_inc(const_ok, 1)
            pool.affine_select(out=before[:], in_=before[:], compare_op=ALU.is_gt, fill=0.0, base=0,
                               pattern=[[1, P]], channel_multiplier=-1).then_inc(const_ok, 1)
            pool.affine_select(out=causal[:, P:S], in_=causal[:, P:S], compare_op=ALU.is_ge, fill=MASKED,
                               base=0, pattern=[[-1, P]], channel_multiplier=1).then_inc(const_ok, 1)
            for t in range(T):
                pool.affine_select(out=cmask[:, t, :], in_=cmask[:, t, :], compare_op=ALU.is_ge, fill=MASKED,
                                   base=t * P - (CMP_LEN - 1), pattern=[[-CMP_STRIDE, 16]],
                                   channel_multiplier=1).then_inc(const_ok, 1)
            pool.affine_select(out=cvalid[:, 0:1], in_=cvalid[:, 0:1], compare_op=ALU.is_ge, fill=0.0,
                               base=-(CMP_LEN - 1), pattern=[[0, 1]], channel_multiplier=1).then_inc(const_ok, 1)
            pool.iota(slot_no[:], pattern=[[1, P]], base=0, channel_multiplier=0,
                      allow_small_or_imprecise_dtypes=True).then_inc(const_ok, 1)
            for layer in range(LAYERS):
                power(T, 24, 2, T, T)
            for layer in range(LAYERS):
                power(T, 4, 12, T, T, T)
            power(T)
        CONST_OK = 7

        @block.tensor
        def _(pe):
            c = Count()

            def piece():
                c.piece += 1
                c.raw += 1
                pe.wait_ge(w_lo, c.piece)
                return c.piece - 1

            def plain(k, n, rows=P):
                pe.wait_ge(w_ld[c.raw % RING], 16 * (c.raw // RING + 1))
                c.raw += 1
                return raw_slot(c.raw - 1, k, n, rows)

            def product(out_, hi, lo, w, wcol, start, stop):
                high, low = (part[wcol] for part in w)
                pe.matmul(out_, hi, high, start=start, stop=False)
                pe.matmul(out_, hi, low, start=False, stop=False)
                return pe.matmul(out_, lo, high, start=False, stop=stop)

            def lin_bank():
                if c.lin >= 4:
                    pe.wait_ge(lin_out, c.lin - 3)
                c.lin += 1
                return 4 + (c.lin - 1) % 4

            def linear(n, late=None):
                banks = [lin_bank() for _ in range(T)]
                for half in range(2):
                    if half == 1 and late:
                        late()
                    w = split_slot(piece(), HALF, n)
                    for t in range(T):
                        normed(half, t)
                        for i in range(HALF):
                            kc = half * HALF + i
                            mm = product(PS[:, banks[t], 0:n], HTh[:, kc, tok(t)], HTl[:, kc, tok(t)], w,
                                         (slice(None), i), kc == 0, kc == KC - 1)
                        if half == 1:
                            mm.then_inc(lin_full, 1)
                    if half == 0:
                        mm.then_inc(w_half, 1)

            def linear_plain(lhs, k, n_all, n):
                w = plain(k, n_all)
                for c0 in range(0, n_all, n):
                    for t in range(T):
                        bank = lin_bank()
                        for kc in range(k):
                            mm = pe.matmul(PS[:, bank, 0:n], lhs(kc, t), w[:, kc, c0:c0 + n],
                                           start=(kc == 0), stop=(kc == k - 1))
                        mm.then_inc(lin_full, 1)

            def turn(batches):
                for srcs, dst, gain in batches:
                    if c.turn >= 4:
                        pe.wait_ge(turn_out, c.turn - 3)
                    off = 0
                    for s in srcs:
                        rows, width = s.shape[0], s.shape[1]
                        mm = pe.transpose(PS[0:width, c.turn % 4, off:off + rows], s, ident[0:rows, 0:rows])
                        off += rows
                    mm.then_inc(turned, 1)
                    c.turn += 1

            def norm(src):
                for b in range(4):
                    half, t = divmod(b, 2)
                    if half == 0:
                        pe.wait_ge(norm_rows, 2 * c.norm + t + 1)
                    for i in range(HALF):
                        kc = half * HALF + i
                        mm = pe.matmul(PS[:, 2 * t + half, i * P:i * P + P], src[:, t, kc * P:kc * P + P], diag[:, t, :],
                                       start=True, stop=True)
                    mm.then_inc(norm_tr, 1)
                c.norm += 1

            def normed(half, t):
                if c.seen < 4 * (c.norm - 1) + 2 * half + t + 1:
                    c.seen = 4 * (c.norm - 1) + 2 * half + t + 1
                    pe.wait_ge(norm_T, c.seen)

            def rows(n=1):
                c.misc += n
                pe.wait_ge(rows_ready, c.misc)

            def attention(units):
                pe.wait_ge(lin_out, c.lin)
                pe.wait_ge(turn_out, c.turn)
                u0 = c.unit
                xs = [c.pt]
                for un in units:
                    xs.append(xs[-1] + len(un["kbs"]))

                def scores(i):
                    u, un = u0 + i, units[i]
                    if u >= 2:
                        pe.wait_ge(sm_ready, u - 1)
                    for m, pairs in enumerate(un["scores"]):
                        for k, (q, key) in enumerate(pairs):
                            mm = pe.matmul(PS[:, 2 * (u % 2) + m // 2, (m % 2) * S:(m % 2) * S + un["kl"]],
                                           q, key, start=(k == 0), stop=(k == len(pairs) - 1))
                    mm.then_inc(sc_full, 1)

                def probs(i):
                    u, un = u0 + i, units[i]
                    pe.wait_ge(p_ready, u + 1)
                    for kb, size in enumerate(un["kbs"]):
                        x = xs[i] + kb
                        if x >= 2:
                            pe.wait_ge(pt_out, x - 1)
                        for m in range(len(un["scores"])):
                            mm = pe.transpose(PS[0:size, 4 + x % 2, m * P:m * P + P],
                                              SM[:, u % 2, m, kb * P:kb * P + size], ident[:])
                        mm.then_inc(pt_full, 1)

                def values(i):
                    u, un = u0 + i, units[i]
                    pe.wait_ge(pt_out, xs[i + 1])
                    if u >= 2:
                        pe.wait_ge(o_out, u - 1)
                    dv = un["dv"]
                    for m, vs in enumerate(un["values"]):
                        for kb, v in enumerate(vs):
                            mm = pe.matmul(PS[:, 6 + u % 2, m * dv:(m + 1) * dv],
                                           PT[0:un["kbs"][kb], u % 2, kb, m, :], v,
                                           start=(kb == 0), stop=(kb == len(vs) - 1))
                    mm.then_inc(o_full, 1)

                for i in range(len(units) + 2):
                    if i < len(units):
                        scores(i)
                    if 1 <= i <= len(units):
                        probs(i - 1)
                    if i >= 2:
                        values(i - 2)
                c.unit += len(units)
                c.pt = xs[-1]
                pe.wait_ge(o_out, c.unit)

            def ffn(chunks, gated):
                parts = 2 if gated else 1

                def hidden(j):
                    for g in range(parts):
                        for half in range(2):
                            w = split_slot(piece(), HALF, 512)
                            for t in range(T):
                                bank = 2 * t + g if gated else 2 * t + j % 2
                                normed(half, t)
                                if g == 1 and half == 0 and j >= 1:
                                    pe.wait_ge(hid_T, c.hid + 2 * (j - 1) + t + 1)
                                for i in range(HALF):
                                    kc = half * HALF + i
                                    mm = product(PS[:, bank, :], HTh[:, kc, tok(t)], HTl[:, kc, tok(t)], w,
                                                 (slice(None), i), kc == 0, kc == KC - 1)
                                if g == parts - 1 and half == 1:
                                    mm.then_inc(hid_full, 1)
                            if not (g == parts - 1 and half == 1):
                                mm.then_inc(w_half, 1)

                def turn_hidden(j):
                    for t in range(T):
                        pe.wait_ge(hid_rows, c.hid + 2 * j + t + 1)
                        bank = 2 * t + 1 if gated else 2 * t + j % 2
                        for i in range(4):
                            mm = pe.transpose(PS[:, bank, i * P:i * P + P], hm[:, t, i * P:i * P + P], ident[:])
                        mm.then_inc(hid_tr, 1)

                def down(j):
                    for half in range(2):
                        w = split_slot(piece(), 2, D)
                        for t in range(T):
                            if half == 0:
                                pe.wait_ge(hid_T, c.hid + 2 * j + t + 1)
                            for i in range(2):
                                k = 2 * half + i
                                for n in range(2):
                                    mm = product(PS[:, 4 + 2 * t + n, :], hTh[:, k, tok(t)], hTl[:, k, tok(t)], w,
                                                 (slice(None), i, slice(n * 512, n * 512 + 512)),
                                                 j == 0 and k == 0, j == chunks - 1 and k == 3)
                            if t == 0 and half == 1 and j == chunks - 1:
                                mm.then_inc(down_first, 1)
                        mm.then_inc(w_half if half == 0 else down_done, 1)

                for j in range(chunks + 1):
                    if j < chunks:
                        hidden(j)
                    if j >= 1:
                        down(j - 1)
                    if j < chunks:
                        turn_hidden(j)
                c.hid += 2 * chunks
                c.down += chunks

            def moe():
                bank = lin_bank()
                normed(1, 1)
                for t in range(T):
                    for kc in range(KC):
                        mm = product(PS[:, bank, t * 8:t * 8 + 8], HTh[:, kc, tok(t)], HTl[:, kc, tok(t)],
                                     (rw_hi, rw_lo), (slice(None), kc), kc == 0, kc == KC - 1)
                mm.then_inc(lin_full, 1)
                bank = lin_bank()
                pe.wait_ge(router_a, 1)
                asg = [rt8[:, t, 0:8] for t in range(T)]
                for col, pairs in ((0, [(before, 0)]), (8, [(ones, 0), (before, 1)]), (16, [(ones, 0), (ones, 1)])):
                    for k, (m_, t) in enumerate(pairs):
                        mm = pe.matmul(PS[:, bank, col:col + 8], m_[:], asg[t], start=(k == 0),
                                       stop=(k == len(pairs) - 1))
                mm.then_inc(lin_full, 1)
                base = c.piece
                pe.wait_ge(routed, 1)
                steps = pe.value_load(nit[0:1, 0:1], min_val=EXPERTS, max_val=2 * EXPERTS)

                def gather():
                    for k in range(KC):
                        for t in range(T):
                            mm = pe.matmul(PS[:, 6 + k // 4, (k % 4) * P:(k % 4) * P + P],
                                           H[:, t, k * P:k * P + P], disp[:, t, :], start=(t == 0), stop=(t == T - 1))
                        if k % 4 == 3:
                            mm.then_inc(e_gath, 1)

                def combine(k):
                    t, half = divmod(k, 2)
                    pe.matmul(PS[:, 6 + k % 2, :], dispT[:, t, :], ye[:, half * 512:half * 512 + 512],
                              start=True, stop=True).then_inc(e_comb, 1)

                pe.wait_ge(e_disp, 1)
                gather()
                with pe.Fori(0, steps) as it:
                    at = [0]

                    def part():
                        at[0] += 1
                        pe.wait_ge(e_lo, it * MOE_PIECES + at[0])
                        return base + at[0] - 1

                    def gate_up(j, g):
                        for half in range(2):
                            w = split_slot(part(), HALF, 512)
                            for i in range(HALF):
                                kc = half * HALF + i
                                mm = product(PS[:, 2 * (j % 2) + g, :], xgh[:, kc, :], xgl[:, kc, :], w,
                                             (slice(None), i), kc == 0, kc == KC - 1)
                            mm.then_inc(e_gu if (g, half) == (1, 1) else e_half, 1)

                    def turn_rows(j):
                        pe.wait_ge(e_rows, it * J1 + (j + 1))
                        for i in range(4):
                            mm = pe.transpose(PS[:, 2 * (j % 2), i * P:i * P + P], hm[:, j % 2, i * P:i * P + P],
                                              ident[:])
                        mm.then_inc(e_tr, 1)

                    def down(j):
                        pe.wait_ge(e_T, it * J1 + (j + 1))
                        for half in range(2):
                            w = split_slot(part(), 2, D)
                            for i in range(2):
                                k = 2 * half + i
                                for n in range(2):
                                    mm = product(PS[:, 4 + n, :], hmh[:, k, :], hml[:, k, :], w,
                                                 (slice(None), i, slice(n * 512, n * 512 + 512)),
                                                 j == 0 and k == 0, j == J1 - 1 and k == 3)
                            mm.then_inc(e_half if half == 0 else e_down, 1)

                    pe.wait_ge(e_xg, it * 2 + 2)
                    gate_up(0, 0)
                    pe.wait_ge(e_y, it * 2 + 2)
                    for k in range(2):
                        combine(k)
                    gate_up(0, 1)
                    for k in range(2, 4):
                        pe.wait_ge(e_acc, it * 4 + (k - 1))
                        combine(k)
                    for j in range(1, J1):
                        gate_up(j, 0)
                        turn_rows(j - 1)
                        if j == 1:
                            pe.wait_ge(e_acc, it * 4 + 3)
                            for t in range(T):
                                mm = pe.transpose(PS[:, 6, t * P:t * P + P], disp[:, t, :], ident[:])
                            mm.then_inc(e_dt, 1)
                        gate_up(j, 1)
                        down(j - 1)
                    turn_rows(J1 - 1)
                    pe.wait_ge(e_disp, it + 2)
                    pe.wait_ge(e_dts, it + 1)
                    pe.wait_ge(e_acc, it * 4 + 4)
                    gather()
                    down(J1 - 1)
                pe.wait_ge(e_y, steps * 2 + 2)
                pe.wait_ge(e_xg, steps * 2 + 2)
                for k in range(4):
                    if k >= 2:
                        pe.wait_ge(e_acc, steps * 4 + (k - 1))
                    combine(k)
                pe.wait_ge(e_acc, steps * 4 + 4)

            pe.wait_ge(const_ok, CONST_OK)
            pe.wait_ge(const_ld, 16 * 6)
            for layer in range(LAYERS):
                norm(X)
                for c0, n in IN1_BLOCKS[0:3]:
                    linear(n)
                rows()
                turn(t_conv)
                for c0, n in IN1_BLOCKS[3:]:
                    linear(n)
                pe.wait_ge(lin_out, c.lin)
                turn(t_cmp)
                bank = lin_bank()
                pe.wait_ge(taps_ready, 4 * (layer + 1))
                for j in range(PE_TAPS):
                    mm = pe.matmul(PS[:, bank, 0:S], tap_matrix(j), CT[:, CC - 1, j:j + S], start=(j == 0),
                                   stop=(j == PE_TAPS - 1))
                mm.then_inc(lin_full, 1)
                for v in range(2):
                    bank = lin_bank()
                    pe.wait_ge(blk_ready, layer + 1)
                    for l in range(CMP_LEN):
                        if l % CMP_STRIDE == 0:
                            w = plain(CMP_STRIDE, CMP_HID, HD)
                        mm = pe.matmul(PS[0:2 * NCMP, bank, 0:CMP_HID], kblk[:, v, l, :], w[:, l % CMP_STRIDE, :],
                                       start=(l == 0), stop=(l == CMP_LEN - 1))
                    mm.then_inc(lin_full, 1)
                pe.wait_ge(lin_out, c.lin)
                turn(t_hid)
                bank = lin_bank()
                pe.wait_ge(turn_out, c.turn)
                for v in range(2):
                    for g in range(2):
                        mm = pe.matmul(PS[0:NCMP, bank, (2 * v + g) * HD:(2 * v + g + 1) * HD],
                                       hid[:, v, g * NCMP:(g + 1) * NCMP], cw2[:, layer, v, :], start=True, stop=True)
                mm.then_inc(lin_full, 1)
                rows()
                turn(t_nsa)
                rows()
                turn(t_kc)
                attention(nsa_units())
                bank = lin_bank()
                pe.wait_ge(conv_step, (layer + 1) * len(CONV_OPS))
                for k in range(CC):
                    mm = pe.matmul(PS[:, bank, 0:S], mean_w[:], Y[:, k, :], start=(k == 0), stop=(k == CC - 1))
                mm.then_inc(lin_full, 1)
                turn(t_mix1)
                bank = lin_bank()
                pe.wait_ge(ln_sq, layer + 1)
                for t in range(T):
                    for k in range(CC):
                        mm = pe.matmul(PS[:, bank, t:t + 1], SQ[:, k, tok(t)], mean_w[:, 0:1], start=(k == 0),
                                       stop=(k == CC - 1))
                mm.then_inc(lin_full, 1)
                bank = lin_bank()
                pe.wait_ge(ln_diag, layer + 1)
                mm = pe.matmul(PS[:, bank, 0:S], ones[:], diag[:].rearrange("p t s -> p (t s)"), start=True, stop=True)
                mm.then_inc(lin_full, 1)
                pe.wait_ge(turn_out, c.turn)
                for n in range(2):
                    linear(512, lambda: pe.wait_ge(mixT_ok, layer + 1))
                norm(X)
                if layer == 0:
                    ffn(J1, True)
                else:
                    moe()
            for layer in range(LAYERS):
                norm(X)
                for c0, n in IN2_BLOCKS:
                    linear(n)
                pe.wait_ge(lin_out, c.lin)
                turn(t_diff)
                attention(diff_units())
                rows()
                turn(t_latent(layer))
                pe.wait_ge(turn_out, c.turn)
                linear_plain(lambda kc, t: CQT[:, kc, tok(t)], 2, 576, 288)
                linear_plain(lambda kc, t: CQT[:, 2, tok(t)], 1, 768, 384)
                turn(t_moba)
                attention(moba_units())
                rows(2)
                turn(t_mla)
                attention(mla_units())
                turn(t_mix2)
                pe.wait_ge(turn_out, c.turn)
                for n in range(2):
                    linear(512)
                norm(MEM)
                for n in range(4):
                    linear(512)
                norm(X)
                for n in range(2):
                    linear(512)
                pe.wait_ge(lin_out, c.lin)
                turn(t_cross)
                attention(cross_units())
                turn(t_mix2)
                pe.wait_ge(turn_out, c.turn)
                for n in range(2):
                    linear(512)
                norm(X)
                ffn(J2, False)

        @block.scalar
        def _(act):
            c = Count()
            past_moe = [False]

            def ahead():
                limit = len(raw_of) if past_moe[0] else before_moe
                while c.split < min(c.piece + AHEAD, limit):
                    i = c.split
                    r = raw_of[i]
                    act.wait_ge(w_ld[r % RING], 16 * (r // RING + 1))
                    if i >= SPLITS and not before_moe <= i < before_moe + SPLITS:
                        act.wait_ge(*pe_done[i - SPLITS])
                    n = size_of[i]
                    act.activation(Wh[:, i % SPLITS, 0:n], ring[:, r % RING, 0:n], ACT.Copy).then_inc(w_hi, 1)
                    c.split += 1

            def norm(gains):
                ahead()
                for b in range(4):
                    half, t = divmod(b, 2)
                    act.wait_ge(norm_tr, 4 * c.norm + b + 1)
                    for i in range(HALF):
                        k = half * HALF + i
                        ins = act.activation(HTh[:, k, tok(t)], PS[:, 2 * t + half, i * P:i * P + P], ACT.Copy,
                                             scale=gains[:, k:k + 1])
                    ins.then_inc(norm_hi, 1)
                c.norm += 1

            def turn_mix(batches):
                for srcs, dst, gain in batches:
                    act.wait_ge(turned, c.turn + 1)
                    act.activation(dst, PS[:, c.turn % 4, :].rearrange("p (m s) -> p m s", m=2),
                                   ACT.Copy).then_inc(mix_hi, 1)
                    c.turn += 1

            def take(dst, func=ACT.Copy, n=None, rows=P, more=None):
                c.lin += 1
                act.wait_ge(lin_full, c.lin)
                bank = 4 + (c.lin - 1) % 4
                width = n or dst.shape[-1]
                if more:
                    d2, f2, o2 = more
                    act.activation(dst, PS[0:rows, bank, 0:width], func)
                    return act.activation(d2, PS[0:rows, bank, o2:o2 + d2.shape[-1]], f2).then_inc(lin_out, 1)
                return act.activation(dst, PS[0:rows, bank, 0:width], func).then_inc(lin_out, 1)

            def turn(batches):
                for srcs, dst, gain in batches:
                    act.wait_ge(turned, c.turn + 1)
                    width = srcs[0].shape[1]
                    n = sum(s.shape[0] for s in srcs)
                    src = PS[0:width, c.turn % 4, 0:n].rearrange("p (m s) -> p m s", m=dst.shape[1])
                    if gain is None:
                        act.activation(dst, src, ACT.Copy).then_inc(turn_out, 1)
                    else:
                        act.activation(dst, src, ACT.Copy, scale=gain).then_inc(turn_out, 1)
                    c.turn += 1

            def attention(units):
                u0 = c.unit
                xs = [c.pt]
                for un in units:
                    xs.append(xs[-1] + len(un["kbs"]))

                def exps(i):
                    u, un = u0 + i, units[i]
                    act.wait_ge(sm_ready, u + 1)
                    if u >= 4:
                        act.wait_ge(o_out, u - 3)
                    for m in range(len(un["scores"])):
                        row = SM[:, u % 2, m, 0:un["kl"]]
                        ins = act.activation(row, row, ACT.Exp, bias=nb[:, u % 2, m:m + 1], scale=un["scale"],
                                             accum_out=sums[:, u % 4, m:m + 1])
                    ins.then_inc(p_ready, 1)

                def copies(i):
                    u, un = u0 + i, units[i]
                    n = len(un["scores"])
                    for kb, size in enumerate(un["kbs"]):
                        x = xs[i] + kb
                        act.wait_ge(pt_full, x + 1)
                        if u >= 2:
                            act.wait_ge(o_full, u - 1)
                        act.activation(PT[0:size, u % 2, kb, 0:n, :],
                                       PS[0:size, 4 + x % 2, 0:n * P].rearrange("p (m s) -> p m s", m=n),
                                       ACT.Copy).then_inc(pt_out, 1)

                for i in range(len(units) + 1):
                    if i < len(units):
                        exps(i)
                    if i >= 1:
                        copies(i - 1)
                c.unit += len(units)
                c.pt = xs[-1]

            def ffn(chunks, gated):
                parts = 2 if gated else 1
                p0 = c.piece
                for j in range(chunks):
                    c.piece = p0 + after_hidden(j, parts)
                    ahead()
                    for t in range(T):
                        q = c.hid + 2 * j + t
                        act.wait_ge(hid_full, q + 1)
                        if q >= 2:
                            act.wait_ge(hid_rows, q - 1)
                        bank = 2 * t if gated else 2 * t + j % 2
                        act.activation(sil[:, t, :], PS[:, bank, :], ACT.Silu if gated else ACT.Relu).then_inc(
                            hid_act, 1)
                    if j >= 1:
                        c.piece += 2
                    ahead()
                    for t in range(T):
                        act.wait_ge(hid_tr, c.hid + 2 * j + t + 1)
                        bank = 2 * t + 1 if gated else 2 * t + j % 2
                        act.activation(hTh[:, :, tok(t)], PS[:, bank, :].rearrange("p (k s) -> p k s", k=4),
                                       ACT.Copy).then_inc(hid_hi, 1)
                c.hid += 2 * chunks
                c.down += chunks
                c.piece = p0 + (2 * parts + 2) * chunks
                ahead()

            def moe(gains):
                c.lin += 2
                act.wait_ge(gate_in, 1)
                act.activation(rt8[:, 8, 0:T], rt8[:, 7, 0:T], ACT.Exp).then_inc(gate_ok, 1)
                act.wait_ge(routed, 1)
                steps = act.value_load(nit[0:1, 0:1], min_val=EXPERTS, max_val=2 * EXPERTS)
                base, raw = c.piece, raw_of[-1 + before_moe] + 1
                act.wait_ge(*pe_done[before_moe - 1])

                def high_rows(first):
                    for h in range(2):
                        act.wait_ge(e_gath, first + h)
                        for i in range(HALF):
                            k = h * HALF + i
                            ins = act.activation(xgh[:, k, :], PS[:, 6 + h, i * P:i * P + P], ACT.Copy,
                                                 scale=gains[:, k:k + 1])
                        ins.then_inc(e_xh, 1)

                def output(i):
                    act.wait_ge(e_down, i * J1 + 1)
                    for half in range(2):
                        act.activation(ye[:, half * 512:half * 512 + 512], PS[:, 4 + half, :],
                                       ACT.Copy).then_inc(e_y, 1)

                high_rows(1)
                with act.Fori(0, steps) as it:
                    at = [0]

                    def split_to(n):
                        while at[0] < min(n, MOE_PIECES):
                            i = at[0]
                            act.wait_ge(e_ld[(raw + i) % RING], it * (16 * (MOE_PIECES // RING)) + 16 * (i // RING + 1))
                            if i < SPLITS - 1:
                                act.wait_ge(e_half, it * MOE_HALVES + 1)
                            elif i == SPLITS - 1:
                                act.wait_ge(e_down, it * J1 + 1)
                            else:
                                kind, j, half = expert[i - SPLITS]
                                if kind and half:
                                    act.wait_ge((e_gu, e_down)[kind - 1], it * J1 + (j + kind))
                                else:
                                    act.wait_ge(e_half, it * MOE_HALVES + (1 + halves[i - SPLITS]))
                            act.activation(Wh[:, (base + i) % SPLITS, :], ring[:, (raw + i) % RING, :],
                                           ACT.Copy).then_inc(e_hi, 1)
                            at[0] += 1

                    def silu(j):
                        act.wait_ge(e_gu, it * J1 + (j + 1))
                        if j >= 2:
                            act.wait_ge(e_rows, it * J1 + (j - 1))
                        act.activation(sil[:, j % 2, :], PS[:, 2 * (j % 2), :], ACT.Silu).then_inc(e_act, 1)

                    def high_turned(j):
                        act.wait_ge(e_tr, it * J1 + (j + 1))
                        act.activation(hmh[:], PS[:, 2 * (j % 2), :].rearrange("p (k s) -> p k s", k=4),
                                       ACT.Copy).then_inc(e_th, 1)

                    split_to(AHEAD)
                    output(it)
                    split_to(at_gate_up(0) + AHEAD)
                    silu(0)
                    for j in range(1, J1):
                        split_to(6 * j + AHEAD)
                        high_turned(j - 1)
                        if j == 1:
                            act.wait_ge(e_dt, it + 1)
                            act.activation(dispT[:].rearrange("p t s -> p (t s)"), PS[:, 6, 0:2 * P],
                                           ACT.Copy).then_inc(e_dts, 1)
                        split_to(at_gate_up(j) + AHEAD)
                        silu(j)
                    split_to(MOE_PIECES)
                    high_turned(J1 - 1)
                    high_rows(it * 2 + 3)
                output(steps)

            for layer in range(LAYERS):
                norm(col1(layer, "attn", 8))
                if layer == 0:
                    act.wait_ge(trig_in, 1)
                    act.activation(trig[:].rearrange("p a b -> p (a b)"), red[:].rearrange("p a b -> p (a b)"),
                                   ACT.Sin).then_inc(trig_ok, 1)
                for k, (c0, n) in enumerate(IN1_BLOCKS):
                    c.piece += 2
                    ahead()
                    for t in range(T):
                        if k < 4:
                            take(proj[:, t, c0:c0 + n], ACT.Sigmoid if k == 1 else ACT.Copy)
                        else:
                            take(proj[:, t, c0:c0 + 256], more=(proj[:, t, GATE0:GATE0 + 24], ACT.Sigmoid, 256))
                    if k == 2:
                        turn(t_conv)
                    if k < 4:
                        for j in range(k * PE_TAPS // 4, (k + 1) * PE_TAPS // 4):
                            ins = act.activation(tap_matrix(j), ident[:], ACT.Copy,
                                                 scale=col1(layer, "cw", 1, (CC - 1) * TAPS + j))
                        ins.then_inc(taps_ready, 1)
                turn(t_cmp)
                c.lin += 1
                act.wait_ge(lin_full, c.lin)
                act.activation(Y[:, CC - 1, :], PS[:, 4 + (c.lin - 1) % 4, 0:S], ACT.Identity,
                               bias=col1(layer, "cb", 1, CC - 1)).then_inc(lin_out, 1)
                for v in range(2):
                    take(hid_rows_sb[:, v, :], ACT.Gelu_apprx_tanh, rows=2 * NCMP)
                turn(t_hid)
                take(kc_sb[0:NCMP, :, :].rearrange("p a b -> p (a b)"), rows=NCMP)
                turn(t_nsa)
                turn(t_kc)
                attention(nsa_units())
                c.lin += 3
                turn_mix(t_mix1)
                act.wait_ge(lin_out, c.lin)
                for k in range(CC):
                    for dst in (HTh[:, CC + k, :], Y[:, k, :]):
                        ins = act.activation(dst, Y[:, k, :], ACT.Silu, bias=col1(layer, "lnb", 1, k),
                                             scale=col1(layer, "lng", 1, k))
                    ins.then_inc(mixT_hi, 1)
                c.lin += 4
                c.piece += 4
                norm(col1(layer, "ffn", 8))
                if layer == 0:
                    ffn(J1, True)
                else:
                    moe(col1(layer, "ffn", 8))
                    past_moe[0] = True
            for layer in range(LAYERS):
                norm(col2(layer, "attn", 8))
                act.wait_ge(lam_in, layer + 1)
                act.activation(lam[:, 0:2], lam[:, 0:2], ACT.Exp).then_inc(lam_ok, 1)
                for c0, n in IN2_BLOCKS:
                    c.piece += 2
                    ahead()
                    for t in range(T):
                        take(proj[:, t, c0:c0 + n])
                turn(t_diff)
                attention(diff_units())
                turn(t_latent(layer))
                for half in range(2):
                    for t in range(T):
                        take(QMf[:, t, half * 288:half * 288 + 288])
                for half in range(2):
                    for t in range(T):
                        take(KVH[:, t, half * 384:half * 384 + 384])
                turn(t_moba)
                attention(moba_units())
                turn(t_mla)
                attention(mla_units())
                turn_mix(t_mix2)
                c.lin += 4
                c.piece += 4
                norm(col2(layer, "mem", 8))
                for n in range(4):
                    c.piece += 2
                    ahead()
                    for t in range(T):
                        take(proj[:, t, n * 512:n * 512 + 512])
                norm(col2(layer, "cross", 8))
                for n in range(2):
                    c.piece += 2
                    ahead()
                    for t in range(T):
                        take(CQ[:, t, n * 512:n * 512 + 512])
                turn(t_cross)
                attention(cross_units())
                turn_mix(t_mix2)
                c.lin += 4
                c.piece += 4
                norm(col2(layer, "mlp", 8))
                ffn(J2, False)

        @block.vector
        def _(dve):
            c = Count()
            done = [0]
            past_moe = [False]

            def seq(ins):
                done[0] += 1
                ins.then_inc(dve_seq, 1)
                dve.wait_ge(dve_seq, done[0])

            def power():
                c.pow += 1
                dve.wait_ge(pow_out, c.pow)

            def ahead():
                limit = len(raw_of) if past_moe[0] else before_moe
                while c.split < min(c.piece + AHEAD, limit):
                    i = c.split
                    r, n = raw_of[i], size_of[i]
                    dve.wait_ge(w_hi, i + 1)
                    dve.tensor_tensor(Wl[:, i % SPLITS, 0:n], ring[:, r % RING, 0:n],
                                      Wh[:, i % SPLITS, 0:n].bitcast(F32), ALU.subtract).then_inc(w_lo, 1)
                    c.split += 1

            def low_scaled(dst, src, hi, gains, width):
                for k in range(HALF):
                    ins = dve.scalar_tensor_tensor(out=dst[:, k, :], in0=src[:, k * width:(k + 1) * width],
                                                   scalar=gains[:, k:k + 1], in1=hi[:, k, :].bitcast(F32),
                                                   op0=ALU.mult, op1=ALU.subtract)
                return ins

            def turn_mix(batches, batches_hi):
                for (_, lo, _), (_, hi, _) in zip(batches, batches_hi):
                    c.mix += 1
                    dve.wait_ge(mix_hi, c.mix)
                    dve.tensor_tensor(lo, PS[:, c.turn % 4, :].rearrange("p (m s) -> p m s", m=2),
                                      hi.bitcast(F32), ALU.subtract).then_inc(turn_out, 1)
                    c.turn += 1

            def mean_eps(n, width, meanwhile=None):
                dve.tensor_scalar(st[:, 0:n], st[:, 0:n], 1.0 / width, EPS, ALU.mult, ALU.add).then_inc(pow_in, 1)
                if meanwhile:
                    meanwhile()
                power()

            def square(src, t, n):
                part = slice(n * 512, n * 512 + 512)
                return dve.tensor_tensor_reduce(H[:, t, part], src[:, t, part], src[:, t, part], 1.0, 0.0, ALU.mult,
                                                ALU.add, sumsq[:, n, t:t + 1])

            def powers(src=None):
                if src is not None:
                    for t in range(T):
                        for n in range(2):
                            ins = square(src, t, n)
                    seq(ins)
                seq(dve.tensor_tensor(st[:, 0:T], sumsq[:, 0, :], sumsq[:, 1, :], ALU.add))
                mean_eps(T, D)
                for t in range(T):
                    dve.tensor_scalar(diag[:, t, :], ident[:], rs[:, t:t + 1], None, ALU.mult).then_inc(norm_rows, 1)

            def norm(gains, keep=False):
                ahead()
                for b in range(4):
                    half, t = divmod(b, 2)
                    ks = slice(half * HALF, (half + 1) * HALF)
                    dve.wait_ge(norm_hi, 4 * c.norm + b + 1)
                    low_scaled(HTl[:, ks, tok(t)], PS[:, 2 * t + half, :], HTh[:, ks, tok(t)], gains[:, ks], P).then_inc(norm_T, 1)
                c.norm += 1
                if keep:
                    for t in range(T):
                        dve.tensor_scalar(H[:, t, :], X[:, t, :], rs[:, t:t + 1], None, ALU.mult)

            def bank_of():
                c.lin += 1
                dve.wait_ge(lin_full, c.lin)
                return 4 + (c.lin - 1) % 4

            def add_out():
                for n in range(2):
                    c.piece += 2
                    ahead()
                    for t in range(T):
                        bank = bank_of()
                        row = X[:, t, n * 512:n * 512 + 512]
                        dve.tensor_tensor(row, PS[:, bank, :], row, ALU.add).then_inc(lin_out, 1)
                        dve.wait_ge(lin_out, c.lin)
                        ins = square(X, t, n)
                seq(ins)

            def heads_norm(src, s0, n, width, gain, rs0):
                seq(dve.tensor_tensor(src, src, bc4(rs[:, rs0:rs0 + n][0:src.shape[0]], width), ALU.mult))
                seq(dve.tensor_tensor(src, src, gain.unsqueeze(1).to_broadcast([src.shape[0], n, width]), ALU.mult))

            def rotate(x1, x2, cos, sin, n, half, signal=None):
                p = x1.shape[0]
                r = [rt[0:p, i, 0:n * half].rearrange("p (n h) -> p n h", n=n) for i in range(4)]
                cb = cos.unsqueeze(1).to_broadcast([p, n, half])
                sb_ = sin.unsqueeze(1).to_broadcast([p, n, half])
                dve.tensor_tensor(r[0], x1, cb, ALU.mult)
                dve.tensor_tensor(r[1], x2, sb_, ALU.mult)
                dve.tensor_tensor(r[2], x2, cb, ALU.mult)
                seq(dve.tensor_tensor(r[3], x1, sb_, ALU.mult))
                dve.tensor_tensor(x1, r[0], r[1], ALU.subtract)
                last = dve.tensor_tensor(x2, r[2], r[3], ALU.add)
                if signal is None:
                    seq(last)
                else:
                    last.then_inc(signal, 1)

            def conv_ops(layer, k0, k1):
                for k in range(k0, k1):
                    j, ch = CONV_OPS[k]
                    src = CT[:, ch, j:j + S]
                    w = col1(layer, "cw", 1, ch * TAPS + j)
                    if j == 0:
                        dve.tensor_scalar(Y[:, ch, :], src, w, col1(layer, "cb", 1, ch), ALU.mult,
                                          ALU.add).then_inc(conv_step, 1)
                        continue
                    if (j, ch) != (PE_TAPS, CC - 1):
                        dve.wait_ge(conv_step, layer * len(CONV_OPS) + CONV_OPS.index((j - 1, ch)) + 1)
                    dve.scalar_tensor_tensor(out=Y[:, ch, :], in0=src, scalar=w, in1=Y[:, ch, :],
                                             op0=ALU.mult, op1=ALU.add).then_inc(conv_step, 1)

            def attention(units, between=None):
                u0 = c.unit
                xs = [c.pt]
                for un in units:
                    xs.append(xs[-1] + len(un["kbs"]))

                def mask(i):
                    u, un = u0 + i, units[i]
                    n, kl = len(un["scores"]), un["kl"]
                    dve.wait_ge(sc_full, u + 1)
                    if i >= 2:
                        dve.wait_ge(pt_full, xs[i - 1])
                    raw = PS[:, 2 * (u % 2):2 * (u % 2) + 2, :].rearrange("p b (m s) -> p (b m) s", s=S)[:, 0:n, 0:kl]
                    tile = SM[:, u % 2, 0:n, 0:kl]
                    if un["bias"] is None:
                        seq(dve.tensor_copy(tile, raw))
                    elif un["bias"][0] == "shared":
                        for m in range(n):
                            ins = dve.tensor_tensor_reduce(tile[:, m, :], raw[:, m, :], un["bias"][1], 1.0, -3e38,
                                                           ALU.add, ALU.max, mx[:, u % 2, m:m + 1])
                        seq(ins)
                    else:
                        for m, s in enumerate(un["bias"][2]):
                            ins = dve.scalar_tensor_tensor(out=tile[:, m, :], in0=un["bias"][1], scalar=s,
                                                           in1=raw[:, m, :], op0=ALU.mult, op1=ALU.add)
                        seq(ins)
                    if un["bias"] is None or un["bias"][0] != "shared":
                        seq(dve.tensor_reduce(mx[:, u % 2, 0:n], tile, AX, ALU.max))
                    dve.tensor_scalar(nb[:, u % 2, 0:n], mx[:, u % 2, 0:n], -un["scale"], None,
                                      ALU.mult).then_inc(sm_ready, 1)

                def end(i):
                    u, un = u0 + i, units[i]
                    n, dv, t = len(un["scores"]), un["dv"], un["t"]
                    dve.wait_ge(o_full, u + 1)
                    cf = coef[:, u % 2, 0:n]
                    seq(dve.reciprocal(cf, sums[:, u % 4, 0:n]))
                    o = PS[:, 6 + u % 2, 0:n * dv].rearrange("p (m d) -> p m d", m=n)
                    kind = un["end"]
                    if kind[0] == "plain":
                        dst = H[:, t, kind[1]:kind[1] + n * dv].rearrange("p (m d) -> p m d", m=n)
                        dve.tensor_tensor(dst, o, bc4(cf, dv), ALU.mult).then_inc(o_out, 1)
                    elif kind[0] == "diff":
                        seq(dve.tensor_tensor(cf, cf, lam4[:], ALU.mult))
                        tmp = otmp[:].rearrange("p (m d) -> p m d", m=4)
                        seq(dve.tensor_tensor(tmp, o, bc4(cf, dv), ALU.mult))
                        pair = otmp[:].rearrange("p (h two d) -> p h two d", h=2, two=2)
                        dst = H[:, t, kind[1]:kind[1] + 128].rearrange("p (h d) -> p h d", h=2)
                        dve.tensor_tensor(dst, pair[:, :, 0, :], pair[:, :, 1, :], ALU.add).then_inc(o_out, 1)
                    else:
                        _, br, g = kind
                        gates = proj[:, t, GATE0:GATE0 + 24].rearrange("p (h b) -> p h b", b=3)[
                            :, g * QPK:(g + 1) * QPK, br]
                        seq(dve.tensor_tensor(cf, cf, gates, ALU.mult))
                        dst = H[:, t, g * QPK * HD:(g + 1) * QPK * HD].rearrange("p (m d) -> p m d", m=n)
                        if br == 0:
                            seq(dve.tensor_scalar(cf, cf, cvalid[:, t:t + 1], None, ALU.mult))
                            dve.tensor_tensor(dst, o, bc4(cf, dv), ALU.mult).then_inc(o_out, 1)
                        else:
                            tmp = otmp[:].rearrange("p (m d) -> p m d", m=4)
                            seq(dve.tensor_tensor(tmp, o, bc4(cf, dv), ALU.mult))
                            dve.tensor_tensor(dst, dst, tmp, ALU.add).then_inc(o_out, 1)

                for i in range(len(units) + 2):
                    if i < len(units):
                        mask(i)
                    if between is not None:
                        between(i, len(units) + 2)
                    if i >= 2:
                        end(i - 2)
                c.unit += len(units)
                c.pt = xs[-1]
                dve.wait_ge(o_out, c.unit)

            def ffn(chunks, gated):
                parts = 2 if gated else 1
                p0 = c.piece
                for j in range(chunks):
                    c.piece = p0 + after_hidden(j, parts)
                    ahead()
                    for t in range(T):
                        q = c.hid + 2 * j + t
                        dve.wait_ge(hid_act, q + 1)
                        if q >= 2:
                            dve.wait_ge(hid_tr, q - 1)
                        dve.tensor_tensor(hm[:, t, :], sil[:, t, :], PS[:, 2 * t + 1, :] if gated else sil[:, t, :],
                                          ALU.mult).then_inc(hid_rows, 1)
                    if j >= 1:
                        c.piece += 2
                    ahead()
                    for t in range(T):
                        dve.wait_ge(hid_hi, c.hid + 2 * j + t + 1)
                        bank = 2 * t + 1 if gated else 2 * t + j % 2
                        dve.tensor_tensor(hTl[:, :, tok(t)], PS[:, bank, :].rearrange("p (k s) -> p k s", k=4),
                                          hTh[:, :, tok(t)].bitcast(F32), ALU.subtract).then_inc(hid_T, 1)
                c.hid += 2 * chunks
                c.down += chunks
                c.piece = p0 + (2 * parts + 2) * chunks
                ahead()
                c.ffn += 1
                for t in range(T):
                    if t == 0:
                        dve.wait_ge(down_first, c.ffn)
                    else:
                        dve.wait_ge(down_done, c.down)
                    for half in range(2):
                        row = X[:, t, half * 512:half * 512 + 512]
                        ins = dve.tensor_tensor(row, PS[:, 4 + 2 * t + half, :], row, ALU.add)
                    seq(ins)
                    for half in range(2):
                        ins = square(X, t, half)
                seq(ins)

            def moe(layer):
                dve.memset(rk[:, :, 16:17], 1000.0).then_inc(e_half, 1)
                dve.memset(gate[:, :, 0:1], 0.0)
                dve.memset(dispT[:], 0.0)
                assert c.lin % 4 == 2
                dve.memset(PS[:, 4:6, :], 0.0).then_inc(e_down, 1)
                bank = bank_of()
                lg = rt8[:, 2:4, 0:8]
                dve.tensor_copy(lg, PS[:, bank, 0:16].rearrange("p (t e) -> p t e", t=T)).then_inc(lin_out, 1)
                dve.wait_ge(lin_out, c.lin)
                top = rt8[:, 4:6, 0:8]
                for t in range(T):
                    ins = dve.max(top[:, t, :], lg[:, t, :])
                seq(ins)
                for t in range(T):
                    ins = dve.max_index(idx8[:, t, :], top[:, t, :], lg[:, t, :])
                seq(ins)
                idf = rt8[:, 6, 0:4].rearrange("p (t k) -> p t k", t=T)
                seq(dve.tensor_copy(idf, idx8[:, :, 0:2]))
                for k in range(2):
                    for t in range(T):
                        ins = dve.tensor_scalar(rt8[:, 9 + 2 * k + t, 0:8], slot_no[:, 0:8], idf[:, t, k:k + 1], None,
                                                ALU.is_equal)
                seq(ins)
                dve.tensor_tensor(rt8[:, 0:2, 0:8], rt8[:, 9:11, 0:8], rt8[:, 11:13, 0:8], ALU.add).then_inc(router_a, 1)
                dve.tensor_tensor(rt8[:, 7, 0:T], top[:, :, 1], top[:, :, 0], ALU.subtract).then_inc(gate_in, 1)
                dve.wait_ge(gate_ok, 1)
                seq(dve.tensor_scalar(rt8[:, 13, 0:T], rt8[:, 8, 0:T], 1.0, None, ALU.add))
                seq(dve.reciprocal(rt8[:, 13, 0:T], rt8[:, 13, 0:T]))
                seq(dve.tensor_tensor(rt8[:, 14, 0:T], rt8[:, 8, 0:T], rt8[:, 13, 0:T], ALU.mult))
                for t in range(T):
                    ins = dve.tensor_scalar(gate[:, t, 1:9], rt8[:, 9 + t, 0:8], rt8[:, 13, t:t + 1], None, ALU.mult)
                seq(ins)
                for t in range(T):
                    ins = dve.scalar_tensor_tensor(out=gate[:, t, 1:9], in0=rt8[:, 11 + t, 0:8],
                                                   scalar=rt8[:, 14, t:t + 1], in1=gate[:, t, 1:9],
                                                   op0=ALU.mult, op1=ALU.add)
                seq(ins)
                seq(dve.tensor_copy(gate[:, :, 9:17], gate[:, :, 1:9]))
                bank = bank_of()
                seq(dve.scalar_tensor_tensor(out=rk[:, :, 0:8], in0=rt8[:, 0:2, 0:8], scalar=-1000.0,
                                             in1=PS[:, bank, 0:16].rearrange("p (t e) -> p t e", t=T),
                                             op0=ALU.mult, op1=ALU.add))
                dve.tensor_reduce(rt8[:, 15, 0:1], PS[:, bank, 16:24], AX, ALU.max).then_inc(lin_out, 1)
                dve.wait_ge(lin_out, c.lin)
                seq(dve.tensor_scalar(rk[:, :, 8:16], rk[:, :, 0:8], 1000.0 - SLOTS, None, ALU.add))
                seq(dve.tensor_scalar(rk[:, :, 0:8], rk[:, :, 0:8], 1000.0, None, ALU.add))
                seq(dve.tensor_scalar(rt8[:, 15, 1:2], rt8[:, 15, 0:1], float(SLOTS), 8.0, ALU.is_gt, ALU.mult))
                dve.tensor_scalar(nit[:, 1:2], rt8[:, 15, 1:2], 7.0, None, ALU.add)
                dve.tensor_scalar(nit[:, 0:1], rt8[:, 15, 1:2], 8.0, None, ALU.add).then_inc(routed, 1)
                dve.wait_ge(routed, 1)
                steps = dve.value_load(nit[0:1, 0:1], min_val=EXPERTS, max_val=2 * EXPERTS)
                gains = col1(layer, "ffn", 8)
                base, raw = c.piece, raw_of[before_moe - 1] + 1

                def dispatch(i):
                    for t in range(T):
                        ins = dve.tensor_scalar(disp[:, t, :], slot_no[:], rk[:, t, bass.ds(i, 1)], None, ALU.is_equal)
                    ins.then_inc(e_disp, 1)

                def low_rows(first):
                    for h in range(2):
                        ks = slice(h * HALF, (h + 1) * HALF)
                        dve.wait_ge(e_xh, first + h)
                        low_scaled(xgl[:, ks, :], PS[:, 6 + h, :], xgh[:, ks, :], gains[:, ks], P).then_inc(e_xg, 1)

                def accumulate(k, i):
                    t, half = divmod(k, 2)
                    dve.wait_ge(e_comb, i * 4 + (k + 1))
                    row = X[:, t, half * 512:half * 512 + 512]
                    dve.scalar_tensor_tensor(out=row, in0=PS[:, 6 + k % 2, :], scalar=gate[:, t, bass.ds(i, 1)],
                                             in1=row, op0=ALU.mult, op1=ALU.add).then_inc(e_acc, 1)

                dispatch(0)
                low_rows(1)
                with dve.Fori(0, steps) as it:
                    at = [0]

                    def split_to(n):
                        while at[0] < min(n, MOE_PIECES):
                            i = at[0]
                            dve.wait_ge(e_hi, it * MOE_PIECES + (i + 1))
                            dve.tensor_tensor(Wl[:, (base + i) % SPLITS, :], ring[:, (raw + i) % RING, :],
                                              Wh[:, (base + i) % SPLITS, :].bitcast(F32), ALU.subtract).then_inc(
                                e_lo, 1)
                            at[0] += 1

                    def hidden(j):
                        dve.wait_ge(e_act, it * J1 + (j + 1))
                        if j >= 2:
                            dve.wait_ge(e_tr, it * J1 + (j - 1))
                        dve.tensor_tensor(hm[:, j % 2, :], sil[:, j % 2, :], PS[:, 2 * (j % 2) + 1, :],
                                          ALU.mult).then_inc(e_rows, 1)

                    def low_turned(j):
                        dve.wait_ge(e_th, it * J1 + (j + 1))
                        dve.tensor_tensor(hml[:], PS[:, 2 * (j % 2), :].rearrange("p (k s) -> p k s", k=4),
                                          hmh[:].bitcast(F32), ALU.subtract).then_inc(e_T, 1)

                    split_to(2 + AHEAD)
                    for k in range(2):
                        accumulate(k, it)
                    split_to(at_gate_up(0) + AHEAD)
                    hidden(0)
                    for k in range(2, 4):
                        accumulate(k, it)
                    for j in range(1, J1):
                        split_to(6 * j + AHEAD)
                        low_turned(j - 1)
                        split_to(at_gate_up(j) + AHEAD)
                        hidden(j)
                        if j == 3:
                            dve.wait_ge(e_dt, it + 1)
                            dispatch(it + 1)
                    split_to(MOE_PIECES)
                    low_turned(J1 - 1)
                    low_rows(it * 2 + 3)
                for k in range(4):
                    accumulate(k, steps)
                dve.wait_ge(e_acc, steps * 4 + 4)
                past_moe[0] = True

            def angles():
                seq(dve.tensor_copy(rw_hi[:], router_w))
                dve.tensor_tensor(rw_lo[:], router_w, rw_hi[:].bitcast(F32), ALU.subtract)
                seq(dve.tensor_copy(posf[:, 0:5], posi[:, 0:5]))
                for t in range(T):
                    dve.tensor_scalar(ang[:, t * 8:t * 8 + 8], inv[:, 0:8], posf[:, t:t + 1], None, ALU.mult)
                    dve.tensor_scalar(ang[:, 24 + t * 16:40 + t * 16], inv[:, 8:24], posf[:, 2 + t:3 + t], None, ALU.mult)
                seq(dve.tensor_scalar(ang[:, 16:24], inv[:, 0:8], posf[:, 4:5], None, ALU.mult))
                turns = rt[:, 0:2, 0:56]
                phase = (0.0, float(np.float32(np.pi / 2)))
                magic = 12582912.0
                two_pi = 2.0 * np.pi
                p1 = float(np.float32(6.28125))
                p2 = float(np.float32(np.round((two_pi - p1) * 2 ** 20) / 2 ** 20))
                p3 = float(np.float32(two_pi - p1 - p2))
                for k in range(2):
                    seq(dve.tensor_scalar(turns[:, k, :], ang[:], phase[k], 1.0 / two_pi, ALU.add, ALU.mult))
                seq(dve.tensor_scalar(turns, turns, magic, None, ALU.add))
                seq(dve.tensor_scalar(turns, turns, magic, None, ALU.subtract))
                seq(dve.tensor_copy(red[:], ang[:].unsqueeze(1).to_broadcast([P, 2, 56])))
                for part in (p1, p2, p3):
                    seq(dve.scalar_tensor_tensor(out=red[:], in0=turns, scalar=-part, in1=red[:], op0=ALU.mult,
                                                 op1=ALU.add))
                seq(dve.tensor_scalar(red[:, 1, :], red[:, 1, :], phase[1], None, ALU.add))
                lim = 3.1415925
                dve.tensor_scalar(red[:], red[:], lim, -lim, ALU.min, ALU.max).then_inc(trig_in, 1)
                seq(dve.tensor_copy(dist[:, 0, :], rowi[:]))
                seq(dve.tensor_scalar(dist[:, 1, :], dist[:, 0, :], posf[:, 3:4], None, ALU.subtract))
                seq(dve.tensor_scalar(dist[:, 0, :], dist[:, 0, :], posf[:, 2:3], None, ALU.subtract))
                seq(dve.scalar_tensor_tensor(out=dist[:], in0=dist[:], scalar=-1.0, in1=dist[:], op0=ALU.mult,
                                             op1=ALU.max))
                dve.tensor_tensor(dist[:, 1, :], dist[:, 1, :], causal[:], ALU.subtract)
                seq(dve.tensor_tensor(dist[:, 0, 0:P], dist[:, 0, 0:P], causal[:, P:S], ALU.subtract))
                dve.wait_ge(trig_ok, 1)

            def sin_cos(c0, n):
                return trig[:, 0, c0:c0 + n], trig[:, 1, c0:c0 + n]

            dve.wait_ge(x_ld, 16)
            for t in range(T):
                for n in range(2):
                    ins = square(X, t, n)
            seq(ins)
            dve.wait_ge(const_ok, CONST_OK)
            dve.wait_ge(const_ld, 16 * 6)
            for layer in range(LAYERS):
                powers()
                norm(col1(layer, "attn", 8))
                if layer == 0:
                    angles()
                base = c.lin
                seq(dve.memset(CT[:, :, 0:TAPS - 1], 0.0))
                c.piece += 4
                ahead()
                dve.wait_ge(lin_out, base + 4)
                dve.tensor_tensor(proj[:, :, GLU_A0:GLU_A0 + 512], proj[:, :, GLU_A0:GLU_A0 + 512],
                                  proj[:, :, GLU_G0:GLU_G0 + 512], ALU.mult).then_inc(rows_ready, 1)
                turn_base = c.turn
                taps = len(CONV_OPS)
                given = [0]

                def convolve(n):
                    n = min(n, taps - given[0])
                    conv_ops(layer, given[0], given[0] + n)
                    given[0] += n

                for _ in range(2):
                    c.piece += 2
                    ahead()
                    dve.wait_ge(turn_out, turn_base + 2)
                    convolve(8)
                c.piece += 2
                ahead()
                dve.wait_ge(turn_out, turn_base + 2 + 2)
                for v in range(2):
                    for g in range(2):
                        for h in range(2):
                            src = QT[0:HD, 12 + 2 * v + g, 16 * h:16 * h + 240].rearrange("p (n b) -> p b n", b=16)
                            pe_ = cpos[:, layer, v, 16 * h:16 * h + 16]
                            ins = dve.tensor_tensor(kblk[:, v, 16 * h:16 * h + 16, g * NCMP:(g + 1) * NCMP], src,
                                                    bc4(pe_, NCMP), ALU.add)
                ins.then_inc(blk_ready, 1)
                dve.wait_ge(lin_out, base + 10)
                regions = [(Q0, 8, 0), (KSLC0, 2, 2), (KWIN0, 2, 3)]
                scr_sq = SM[:].rearrange("p a b c -> p (a b c)")
                o = 0
                for t in range(T):
                    for c0, n, gi in regions:
                        view = proj[:, t, c0:c0 + n * HD]
                        sq = scr_sq[:, 0:n * HD]
                        seq(dve.tensor_tensor(sq, view, view, ALU.mult))
                        seq(dve.tensor_reduce(st[:, o:o + n], sq.rearrange("p (h d) -> p h d", d=HD), AX, ALU.add))
                        o += n
                mean_eps(24, HD, lambda: convolve(10))
                o = 0
                for t in range(T):
                    sin, cos = sin_cos(t * 8, 8)
                    for c0, n, gi in regions:
                        view = proj[:, t, c0:c0 + n * HD].rearrange("p (h d) -> p h d", d=HD)
                        gain = bc[:, layer * B1W + gi * HD:layer * B1W + (gi + 1) * HD]
                        heads_norm(view, 0, n, HD, gain, o)
                        o += n
                        rotate(view[:, :, 0:8], view[:, :, 8:16], cos, sin, n, 8,
                               rows_ready if o == 24 else None)
                convolve(20)
                dve.wait_ge(lin_out, base + 14)
                kk = kc_sb[0:NCMP, 0:2, :]
                sq = scr_sq[0:NCMP, 0:2 * HD].rearrange("p (h d) -> p h d", d=HD)
                seq(dve.tensor_tensor(sq, kk, kk, ALU.mult))
                seq(dve.tensor_reduce(st[0:NCMP, 0:2], sq, AX, ALU.add))
                mean_eps(2, HD)
                heads_norm(kk, 0, 2, HD, bc[0:NCMP, layer * B1W + HD:layer * B1W + 2 * HD], 0)
                sin, cos = sin_cos(16, 8)
                rotate(kk[:, :, 0:8], kk[:, :, 8:16], cos[0:NCMP, :], sin[0:NCMP, :], 2, 8, rows_ready)

                early = given[0]

                def between(i, n):
                    convolve((taps - early) * (i + 1) // n - (taps - early) * i // n)

                c.turn += 2 + 2 + 1 + 6 + 1
                attention(nsa_units(), between)
                c.lin = base + 14
                bank = bank_of()
                mean = PS[:, bank, 0:S].unsqueeze(1).to_broadcast([P, CC, S])
                dve.tensor_tensor(Y, Y, mean, ALU.subtract).then_inc(lin_out, 1)
                dve.wait_ge(lin_out, c.lin)
                dve.tensor_tensor(SQ, Y, Y, ALU.mult).then_inc(ln_sq, 1)
                turn_mix(t_mix1_lo, t_mix1)
                bank = bank_of()
                dve.tensor_scalar(st[:, 0:T], PS[:, bank, 0:T], EPS, None, ALU.add).then_inc(pow_in, 1)
                power()
                for t in range(T):
                    dve.tensor_scalar(diag[:, t, :], ident[:], rs[:, t:t + 1], None, ALU.mult).then_inc(
                        (lin_out, ln_diag)[t], 1)
                bank = bank_of()
                dve.tensor_tensor(Y, Y, PS[:, bank, 0:S].unsqueeze(1).to_broadcast([P, CC, S]),
                                  ALU.mult).then_inc(lin_out, 1)
                ahead()
                for k in range(CC):
                    dve.wait_ge(mixT_hi, layer * CC + k + 1)
                    ins = dve.tensor_tensor(HTl[:, CC + k, :], Y[:, k, :], HTh[:, CC + k, :].bitcast(F32), ALU.subtract)
                ins.then_inc(mixT_ok, 1)
                add_out()
                powers()
                norm(col1(layer, "ffn", 8), keep=layer == 1)
                if layer == 0:
                    ffn(J1, True)
                else:
                    moe(layer)

            for layer in range(LAYERS):
                powers(X if layer == 0 else None)
                norm(col2(layer, "attn", 8))
                base = c.lin
                b0 = 2 * B1W + layer * B2W
                for k in range(2):
                    lq, lk = (bc[:, b0 + HD + (2 * k + i) * DIFF_D:b0 + HD + (2 * k + i + 1) * DIFF_D] for i in range(2))
                    seq(dve.tensor_tensor_reduce(rt[:, k, 0:DIFF_D], lq, lk, 1.0, 0.0, ALU.mult, ALU.add,
                                                 lam[:, k:k + 1]))
                dve.tensor_copy(lam[:, 2:4], mhalf[:].to_broadcast([P, 2])).then_inc(lam_in, 1)
                dve.wait_ge(lam_ok, layer + 1)
                lam0 = 0.8 - 0.6 * float(np.exp(-0.3 * layer))
                seq(dve.tensor_tensor(lam[:, 2:3], lam[:, 1:2], lam[:, 0:1], ALU.subtract))
                seq(dve.memset(lam4[:], 1.0))
                for k in (1, 3):
                    ins = dve.tensor_scalar(lam4[:, k:k + 1], lam[:, 2:3], -lam0, None, ALU.add)
                seq(ins)
                c.piece += 2
                ahead()
                dve.wait_ge(lin_out, base + 2)
                parts = [(t, c0, n, 2 * t + i) for t in range(T) for i, (c0, n) in enumerate(((0, QR), (CKV0, KVR)))]
                junk = SM[:].rearrange("p a b c -> p (a b c)")
                for t, c0, n, o in parts:
                    view = proj[:, t, c0:c0 + n]
                    seq(dve.tensor_tensor_reduce(junk[:, 0:n], view, view, 1.0 / n, 0.0, ALU.mult, ALU.add,
                                                 st[:, o:o + 1]))
                mean_eps(4, 1)
                for t, c0, n, o in parts:
                    view = proj[:, t, c0:c0 + n]
                    ins = dve.tensor_scalar(view, view, rs[:, o:o + 1], None, ALU.mult)
                ins.then_inc(rows_ready, 1)
                c.piece += 8
                ahead()
                attention(diff_units())
                for t in range(T):
                    view = H[:, t, 384:768]
                    seq(dve.tensor_tensor(junk[:, 0:384], view, view, ALU.mult))
                    seq(dve.tensor_reduce(st[:, 6 * t:6 * t + 6], junk[:, 0:384].rearrange("p (h d) -> p h d", d=64),
                                          AX, ALU.add))
                mean_eps(12, 64)
                seq(dve.tensor_scalar(rs[:, 0:12], rs[:, 0:12], 1.0 - lam0, None, ALU.mult))
                for t in range(T):
                    view = H[:, t, 384:768].rearrange("p (h d) -> p h d", d=64)
                    seq(dve.tensor_tensor(view, view, bc4(rs[:, 6 * t:6 * t + 6], 64), ALU.mult))
                    ins = dve.tensor_tensor(view, view, bc[:, b0:b0 + 64].unsqueeze(1).to_broadcast([P, 6, 64]), ALU.mult)
                ins.then_inc(rows_ready, 1)
                dve.wait_ge(lin_out, base + 18)
                for t in range(T):
                    sin, cos = sin_cos(24 + 16 * t, 16)
                    kr = proj[:, t, KR0:KR0 + MROPE].unsqueeze(1)
                    rotate(kr[:, :, 0:16], kr[:, :, 16:32], cos, sin, 1, 16)
                    q = QM[:, t, :, :]
                    rotate(q[:, :, NOPE:NOPE + 16], q[:, :, NOPE + 16:NOPE + 32], cos, sin, MLA_H, 16,
                           rows_ready if t == T - 1 else None)
                attention(moba_units())
                attention(mla_units())
                c.lin = base + 18
                c.turn += len(t_latent(layer)) + len(t_mla) + len(t_diff) + len(t_moba)
                turn_mix(t_mix2_lo, t_mix2)
                dve.wait_ge(mem_ld, 16 * (layer + 1))
                powers(MEM)
                add_out()
                norm(col2(layer, "mem", 8))
                c.piece += 8
                powers()
                norm(col2(layer, "cross", 8))
                c.piece += 4
                ahead()
                attention(cross_units())
                c.lin += 12
                c.turn += len(t_cross)
                turn_mix(t_mix2_lo, t_mix2)
                add_out()
                powers()
                norm(col2(layer, "mlp", 8))
                ffn(J2, False)
            seq(dve.tensor_tensor(st[:, 0:T], sumsq[:, 0, :], sumsq[:, 1, :], ALU.add))
            mean_eps(T, D)
            dve.wait_ge(fin_ld, 16)
            for t in range(T):
                dve.scalar_tensor_tensor(out=H[:, t, :], in0=X[:, t, :], scalar=rs[:, t:t + 1], in1=MEM[:, 0, :],
                                         op0=ALU.mult, op1=ALU.mult).then_inc(x_done, 1)


WEIGHTS = ["w_in", "w_out", "cmp_w1_k", "cmp_w1_v", "ffn_w_gate", "ffn_w_up", "ffn_w_down", "moe_w_gate", "moe_w_up",
           "moe_w_down", "w_in_2", "mla_w_uq_2", "mla_w_ukv_2", "w_out_2", "cross_wq_2", "cross_wkv_2", "cross_wo_2",
           "mlp_w1_2", "mlp_w2_2", "x", "mem_2", "positions_2", "final_norm_2"]


def by_partition(v):
    return v.reshape(-1, P).T


def kernel(**inputs):
    import concourse.bacc as bacc
    from concourse.bass_utils import run_bass_kernel_spmd

    x = {k: np.asarray(v) for k, v in inputs.items()}
    arrays = {k: np.ascontiguousarray(x[k]) for k in WEIGHTS}
    arrays["final_norm_2"] = arrays["final_norm_2"].reshape(1, D)
    cols = []
    for l in range(LAYERS):
        cols += [by_partition(x[k][l]) for k in ("attn_norm_g", "ffn_norm_g", "conv_b", "conv_ln_g", "conv_ln_b")]
        cols.append(x["conv_w"][l].reshape(TAPS, CC, P).transpose(2, 1, 0).reshape(P, CC * TAPS))
    for l in range(LAYERS):
        cols += [by_partition(x[k][l]) for k in ("attn_norm_2", "cross_norm_2", "mem_norm_2", "mlp_norm_2",
                                                 "mla_q_norm_2", "mla_kv_norm_2")]
    cols.append(x["moe_router"][0].reshape(KC, P, EXPERTS).transpose(1, 0, 2).reshape(P, KC * EXPERTS))
    arrays["cols"] = np.ascontiguousarray(np.concatenate(cols, axis=1))
    rows = []
    for l in range(LAYERS):
        rows += [x["q_norm_g"][l], x["k_norm_g"][l].reshape(-1)]
    for l in range(LAYERS):
        rows += [x["diff_sub_norm_2"][l]] + [x[f"diff_lambda_{k}_2"][l] for k in ("q1", "k1", "q2", "k2")]
    arrays["bc"] = np.ascontiguousarray(np.concatenate(rows)[None, :])
    arrays["cpos"] = np.ascontiguousarray(
        np.stack([x["cmp_pos_k"], x["cmp_pos_v"]], axis=1).transpose(3, 0, 1, 2))
    arrays["cw2"] = np.ascontiguousarray(np.stack([x["cmp_w2_k"], x["cmp_w2_v"]], axis=1).transpose(2, 0, 1, 3))
    posc = np.zeros((P, 5), np.int32)
    posc[:, 0:2] = by_partition(x["positions"][0])
    posc[:, 2:4] = by_partition(x["positions_2"][0])
    posc[0:NCMP, 4] = x["positions"][0, CMP_LEN - 1::CMP_STRIDE]
    arrays["posc"] = posc

    nc = bacc.Bacc("TRN2", target_bir_lowering=False, num_devices=1, dynamic_dma_scratch_size=1024)
    aps = {k: nc.dram_tensor(f"in_{k}", v.shape, mybir.dt.from_np(v.dtype), kind="ExternalInput").ap()
           for k, v in arrays.items()}
    out = nc.dram_tensor("out_0", (1, S, D), F32, kind="ExternalOutput").ap()
    build(nc, aps, out)
    r = run_bass_kernel_spmd(nc, [{f"in_{k}": v for k, v in arrays.items()}], core_ids=[0])
    return r.results[0]["out_0"]
```
